# Optimizing a Trainium2 kernel written in Bass

```python
import math
import jax, jax.numpy as jnp
from jax import lax
import numpy as np

D_MODEL = 2048
BATCH = 1
SEQ = 512
DEPTH = 1

N_Q_HEADS = 16
N_KV_HEADS = 4
HEAD_DIM = 64
GROUP = N_Q_HEADS // N_KV_HEADS
ATTN_WIDTH = N_Q_HEADS * HEAD_DIM
KV_WIDTH = N_KV_HEADS * HEAD_DIM
WINDOW = 128
BLOCK = WINDOW
N_BUCKETS = 32
MAX_DISTANCE = 128
RNN_WIDTH = D_MODEL
RNN_BLOCKS = 16
RNN_BLOCK_DIM = RNN_WIDTH // RNN_BLOCKS
CONV_WIDTH = 4
LRU_C = 8.0
SPLITS = (ATTN_WIDTH, KV_WIDTH, KV_WIDTH, ATTN_WIDTH, RNN_WIDTH, RNN_WIDTH, D_MODEL, D_MODEL)
IN_WIDTH = sum(SPLITS)
SPLIT_POINTS = np.cumsum(SPLITS)[:-1].tolist()
DEEPNORM_ALPHA = (2.0 * DEPTH) ** 0.25
DEEPNORM_BETA = (8.0 * DEPTH) ** -0.25
LN_EPS = 1e-5
NEG_INF = -1e30

kernel_name = "hybrid_swa_sink_rglru_gated_deepnorm"

def t5_causal_bucket(dist):
    max_exact = N_BUCKETS // 2
    n = jnp.maximum(dist, 0)
    nf = jnp.maximum(n, max_exact).astype(jnp.float32)
    large = max_exact + (jnp.log(nf / max_exact) / math.log(MAX_DISTANCE / max_exact)
                         * (N_BUCKETS - max_exact)).astype(jnp.int32)
    large = jnp.minimum(large, N_BUCKETS - 1)
    return jnp.where(n < max_exact, n, large)

def layer_norm(x, g, b):
    xf = x.astype(jnp.float32)
    mu = xf.mean(-1, keepdims=True)
    var = jnp.square(xf - mu).mean(-1, keepdims=True)
    return ((xf - mu) * lax.rsqrt(var + LN_EPS) * g.astype(jnp.float32)
            + b.astype(jnp.float32)).astype(x.dtype)

def sliding_window_attention(q, k, v, sinks, rel_bias):
    B, S = q.shape[:2]
    nb = S // BLOCK
    qb = q.reshape(B, nb, BLOCK, N_KV_HEADS, GROUP, HEAD_DIM)
    pad = jnp.zeros((B, BLOCK, N_KV_HEADS, HEAD_DIM), k.dtype)

    def band(t):
        tp = jnp.concatenate([pad, t], axis=1).reshape(B, nb + 1, BLOCK, N_KV_HEADS, HEAD_DIM)
        return jnp.concatenate([tp[:, :-1], tp[:, 1:]], axis=2)

    kband, vband = band(k), band(v)
    s = jnp.einsum('bnqkgd,bnskd->bnkgqs', qb, kband).astype(jnp.float32) * (HEAD_DIM ** -0.5)

    qi = jnp.arange(BLOCK)[:, None]
    kj = jnp.arange(2 * BLOCK)[None, :]
    dist = qi + BLOCK - kj
    bias = rel_bias[t5_causal_bucket(dist)].astype(jnp.float32)
    bias = bias.transpose(2, 0, 1).reshape(N_KV_HEADS, GROUP, BLOCK, 2 * BLOCK)
    in_window = (dist >= 0) & (dist < WINDOW)
    key_pos = jnp.arange(nb)[:, None] * BLOCK + kj - BLOCK
    valid = in_window[None] & (key_pos >= 0)[:, None, :]
    s = jnp.where(valid[None, :, None, None], s + bias, NEG_INF)

    sink = sinks.astype(jnp.float32).reshape(N_KV_HEADS, GROUP)[None, None, :, :, None, None]
    m = jnp.maximum(s.max(-1, keepdims=True), sink)
    p = jnp.exp(s - m)
    denom = p.sum(-1, keepdims=True) + jnp.exp(sink - m)
    p = (p / denom).astype(v.dtype)
    o = jnp.einsum('bnkgqs,bnskd->bnqkgd', p, vband)
    return o.reshape(B, S, ATTN_WIDTH)

def causal_depthwise_conv(x, w, b):
    y = lax.conv_general_dilated(x, w[:, None, :], window_strides=(1,),
                                 padding=[(CONV_WIDTH - 1, 0)],
                                 dimension_numbers=('NWC', 'WIO', 'NWC'),
                                 feature_group_count=x.shape[-1])
    return y + b

def rg_lru(x, w_r, b_r, w_i, b_i, lam):
    B, S, _ = x.shape
    xb = x.reshape(B, S, RNN_BLOCKS, RNN_BLOCK_DIM)
    r = jax.nn.sigmoid(jnp.einsum('bshi,hij->bshj', xb, w_r).reshape(B, S, RNN_WIDTH) + b_r)
    i = jax.nn.sigmoid(jnp.einsum('bshi,hij->bshj', xb, w_i).reshape(B, S, RNN_WIDTH) + b_i)
    log_a = -LRU_C * r.astype(jnp.float32) * jax.nn.softplus(-lam.astype(jnp.float32))
    a = jnp.exp(log_a)
    u = jnp.sqrt(-jnp.expm1(2.0 * log_a)) * (i * x).astype(jnp.float32)

    def combine(left, right):
        a_l, h_l = left
        a_r, h_r = right
        return a_l * a_r, a_r * h_l + h_r

    _, h = lax.associative_scan(combine, (a, u), axis=1)
    return h.astype(x.dtype)

def hybrid_layer(x, w_in, conv_w, conv_b, w_r, b_r, w_i, b_i, lru_lambda, sinks,
                 w_attn_out, w_rnn_out, w_out, ln_g, ln_b, rel_bias):
    B, S, _ = x.shape
    proj = x @ w_in
    q, k, v, g_attn, x_rnn, g_rnn, m_attn, m_rnn = jnp.split(proj, SPLIT_POINTS, axis=-1)
    attn = sliding_window_attention(q.reshape(B, S, N_Q_HEADS, HEAD_DIM),
                                    k.reshape(B, S, N_KV_HEADS, HEAD_DIM),
                                    v.reshape(B, S, N_KV_HEADS, HEAD_DIM),
                                    sinks, rel_bias)
    y_attn = (attn * jax.nn.silu(g_attn)) @ w_attn_out
    h = rg_lru(causal_depthwise_conv(x_rnn, conv_w, conv_b), w_r, b_r, w_i, b_i, lru_lambda)
    y_rnn = (h * jax.nn.silu(g_rnn)) @ w_rnn_out
    mixed = jax.nn.sigmoid(m_attn) * y_attn + jax.nn.sigmoid(m_rnn) * y_rnn
    out = mixed @ w_out
    return layer_norm(DEEPNORM_ALPHA * x + out, ln_g, ln_b)

def setup_inputs(seed: int = 0) -> dict:
    key = jax.random.key(seed)
    ks = jax.random.split(key, 16)
    f32 = jnp.float32
    x = jax.random.normal(ks[0], (BATCH, SEQ, D_MODEL), f32)
    w_in = jax.random.normal(ks[1], (DEPTH, D_MODEL, IN_WIDTH), f32) * D_MODEL ** -0.5
    conv_w = jax.random.normal(ks[2], (DEPTH, CONV_WIDTH, RNN_WIDTH), f32) * CONV_WIDTH ** -0.5
    conv_b = jax.random.normal(ks[3], (DEPTH, RNN_WIDTH), f32) * 0.01
    w_r = jax.random.normal(ks[4], (DEPTH, RNN_BLOCKS, RNN_BLOCK_DIM, RNN_BLOCK_DIM), f32) * RNN_BLOCK_DIM ** -0.5
    b_r = jax.random.normal(ks[5], (DEPTH, RNN_WIDTH), f32) * 0.01
    w_i = jax.random.normal(ks[6], (DEPTH, RNN_BLOCKS, RNN_BLOCK_DIM, RNN_BLOCK_DIM), f32) * RNN_BLOCK_DIM ** -0.5
    b_i = jax.random.normal(ks[7], (DEPTH, RNN_WIDTH), f32) * 0.01
    u = jax.random.uniform(ks[8], (DEPTH, RNN_WIDTH), f32, minval=0.9, maxval=0.999)
    a = u ** (1.0 / LRU_C)
    lru_lambda = jnp.log(a) - jnp.log1p(-a)
    sinks = jax.random.normal(ks[9], (DEPTH, N_Q_HEADS), f32) * 0.5
    w_attn_out = jax.random.normal(ks[10], (DEPTH, ATTN_WIDTH, D_MODEL), f32) * ATTN_WIDTH ** -0.5
    w_rnn_out = jax.random.normal(ks[11], (DEPTH, RNN_WIDTH, D_MODEL), f32) * RNN_WIDTH ** -0.5
    w_out = jax.random.normal(ks[12], (DEPTH, D_MODEL, D_MODEL), f32) * (D_MODEL ** -0.5) * DEEPNORM_BETA
    ln_g = 1.0 + 0.02 * jax.random.normal(ks[13], (DEPTH, D_MODEL), f32)
    ln_b = 0.02 * jax.random.normal(ks[14], (DEPTH, D_MODEL), f32)
    rel_bias = jax.random.normal(ks[15], (N_BUCKETS, N_Q_HEADS), f32) * 0.5
    return {"x": x, "w_in": w_in, "conv_w": conv_w, "conv_b": conv_b, "w_r": w_r, "b_r": b_r,
            "w_i": w_i, "b_i": b_i, "lru_lambda": lru_lambda, "sinks": sinks,
            "w_attn_out": w_attn_out, "w_rnn_out": w_rnn_out, "w_out": w_out,
            "ln_g": ln_g, "ln_b": ln_b, "rel_bias": rel_bias}

def reference(x, w_in, conv_w, conv_b, w_r, b_r, w_i, b_i, lru_lambda, sinks,
              w_attn_out, w_rnn_out, w_out, ln_g, ln_b, rel_bias):
    for l in range(DEPTH):
        x = hybrid_layer(x, w_in[l], conv_w[l], conv_b[l], w_r[l], b_r[l], w_i[l], b_i[l],
                         lru_lambda[l], sinks[l], w_attn_out[l], w_rnn_out[l], w_out[l],
                         ln_g[l], ln_b[l], rel_bias)
    return x


_drawn_inputs = setup_inputs


def setup_inputs(seed=0):
    import zlib

    import numpy as np

    out = dict(_drawn_inputs(seed))
    spreads = {}
    factors = {'conv_b': 8.0,
     'b_r': 200.0,
     'b_i': 64.0,
     'sinks': 29.524,
     'ln_g': 21.41,
     'ln_b': 21.5,
     'rel_bias': 4.46}
    for name, (base, spread) in spreads.items():
        noise = np.random.default_rng([zlib.crc32(name.encode()), seed]).standard_normal(out[name].shape)
        drawn = base * np.exp(spread * noise) if base else spread * noise
        out[name] = __import__('jax').numpy.asarray(drawn.astype(out[name].dtype))
    for name, factor in factors.items():
        out[name] = (out[name] * factor).astype(out[name].dtype)
    return out
```

```python
from contextlib import ExitStack

import concourse.bass as bass
from concourse import mybir

F32 = mybir.dt.float32
F32R = mybir.dt.float32r
ALU = mybir.AluOpType
ACT = mybir.ActivationFunctionType
AX = mybir.AxisListType

P = 128
NEG_INF = -1e30
LN_EPS = 1e-5
LRU_C = 8.0
DEPTH = 1
ALPHA = (2.0 * DEPTH) ** 0.25


def hybrid_layer(nc, x_t, x, w_in, chan, w_r, w_i, sinks, w_attn_out, w_rnn_out, w_out,
                 ln_g, ln_b, rel_bias, bucket_rows, out):
    D, S = x_t.shape
    KT = D // P
    HEADS = sinks.shape[1]
    HD = w_attn_out.shape[1] // HEADS
    KV_HEADS = 4
    GROUP = HEADS // KV_HEADS
    NB = S // P
    AT = HEADS * HD // P
    KVT = KV_HEADS * HD // P
    ITEMS = NB * KV_HEADS
    assert GROUP == 4 and HD == 64 and S == 512 and KT == 16 and ITEMS == KT
    SCALE = HD ** -0.5
    BUCKETS = rel_bias.shape[0]
    SPAN = bucket_rows.shape[1]

    COL_Q = 0
    COL_KV = COL_Q + AT * P
    COL_GA = COL_KV + 2 * KVT * P
    COL_X = COL_GA + AT * P
    COL_GR = COL_X + D
    COL_MA = COL_GR + D
    COL_MR = COL_MA + D

    T_KV = 0
    T_QG = T_KV + 2 * KVT
    T_MA = T_QG + 2 * AT
    T_AO = T_MA + KT
    T_RN = T_AO + KT // 2
    T_MX = T_RN + 2 * KT
    T_WO = T_MX + 2 * KT
    A_QG = KVT
    A_MA = A_QG + AT
    A_AO = A_MA + KT
    A_RN = A_AO + KT // 2
    A_MX = A_RN + KT
    B_QG = KVT
    B_AO = B_QG + AT
    B_RN = B_AO + KT // 2
    B_MX = B_RN + KT

    w_in_v = w_in[0].rearrange("(k p) n -> p k n", p=P)
    w_ao_v = w_attn_out[0].rearrange("(k p) n -> p k n", p=P)
    w_ro_v = w_rnn_out[0].rearrange("(k p) n -> p k n", p=P)
    w_out_v = w_out[0].rearrange("(k p) n -> p k n", p=P)
    w_r_v = w_r[0].rearrange("h i j -> i h j")
    w_i_v = w_i[0].rearrange("h i j -> i h j")
    x_t_v = x_t.rearrange("(k p) s -> p k s", p=P)
    x_v = x[0].rearrange("(b p) d -> p b d", p=P)
    out_v = out[0].rearrange("(b p) d -> p b d", p=P)
    ds = bass.ds

    with ExitStack() as ctx:
        def sb(name, shape, dt=F32, where=ctx):
            return where.enter_context(nc.sbuf_tensor(name, shape, dt))

        def sem(name):
            return ctx.enter_context(nc.semaphore(name))

        def ps(name, shape):
            return ctx.enter_context(nc.psum_tensor(name, shape, F32))

        bias_rows_d = nc.dram_tensor("bias_rows", [HEADS, P, SPAN], F32, kind="Internal").ap()

        xt_hi = sb("xt_hi", [P, KT, S], F32R)
        xt_lo = sb("xt_lo", [P, KT, S], F32R)
        merged = sb("merged", [P, KT, S])
        raw = sb("raw", [P, 2, 8, P])
        w_hi = sb("w_hi", [P, 4, 4, P], F32R)
        w_lo = sb("w_lo", [P, 4, 4, P], F32R)
        gate_w = sb("gate_w", [P, 2, P])
        chan_sb = sb("chan_sb", [P, KT, 8])
        ident = sb("ident", [P, P])
        neg_sinks = sb("neg_sinks", [P, HEADS])
        exp_scale = sb("exp_scale", [P, KT])
        tanh_scale = sb("tanh_scale", [P, KT])
        small = sb("small", [P, 6, 4])
        stats = sb("stats", [P, NB, 4, 6])
        moments = sb("moments", [P, NB, 2])
        spread = sb("spread", [P, NB, 2])

        early = ExitStack()
        q_sb = sb("q_sb", [P, NB, AT * P], where=early)
        bias = sb("bias", [P, HEADS, 2 * P], where=early)
        g_attn = sb("g_attn", [P, NB, AT * P], where=early)
        k_sb = sb("k_sb", [P, KV_HEADS, S], where=early)
        v_sb = sb("v_sb", [P, NB, KV_HEADS * HD], where=early)
        sb("pad", [P, 1024], where=early)
        probs = sb("probs", [P, GROUP, 2 * P], where=early)
        probs_t = sb("probs_t", [P, 2, GROUP * P], where=early)
        q_item = sb("q_item", [P, 2 * P], where=early)
        k_item = sb("k_item", [P, 2 * P], where=early)
        v_item = sb("v_item", [P, 2, HD], where=early)
        sig_qg = sb("sig_qg", [P, S], where=early)
        v_t = sb("v_t", [P, KVT, S], where=early)
        sinks_sb = sb("sinks_sb", [P, HEADS], where=early)
        table_sb = sb("table_sb", [BUCKETS, HEADS], where=early)
        bias_table = sb("bias_table", [BUCKETS + 1, HEADS], where=early)
        buckets = sb("buckets", [BUCKETS + 1, SPAN], where=early)
        bias_rows = sb("bias_rows_sb", [HEADS, SPAN], where=early)
        sp = sb("sp", [P, 6, KT], where=early)
        early.close()

        hg_hi = sb("hg_hi", [P, KT, S], F32R)
        hg_lo = sb("hg_lo", [P, KT, S], F32R)
        middle = ExitStack()
        xc = sb("xc", [P, S], where=middle)
        rec_gate = sb("rec_gate", [P, S], where=middle)
        inp = sb("inp", [P, S], where=middle)
        decay = sb("decay", [P, S], where=middle)
        norm = sb("norm", [P, S], where=middle)
        hid = sb("hid", [P, S], where=middle)
        silu = sb("silu", [P, S], where=middle)
        gated = sb("gated", [P, S], where=middle)
        middle.close()
        ln_gb = sb("ln_gb", [P, 2, D])
        sig_mr = sb("sig_mr", [P, S])
        mixed_r = sb("mixed_r", [P, S])
        ag_hi, ag_lo = hg_hi[:, 0:AT, :], hg_hi[:, AT:2 * AT, :]

        bank_a = ps("bank_a", [P, S])
        bank_b = ps("bank_b", [P, S])
        bank_s = ps("bank_s", [P, 2, S])
        bank_t = ps("bank_t", [P, 2, S])
        bank_o = ps("bank_o", [P, S])
        scores = bank_s[:, :, :].rearrange("p a (h k) -> p (a h) k", h=2)
        out_banks = [bank_s[:, 0, :], bank_s[:, 1, :], bank_t[:, 0, :], bank_t[:, 1, :]]

        raw_landed = [sem("raw_landed0"), sem("raw_landed1")]
        hi_ready = sem("hi_ready")
        lo_ready = sem("lo_ready")
        multiplied = sem("multiplied")
        a_free = sem("a_free")
        b_free = sem("b_free")
        X_CUTS = [0, 2, 4, 8, 16]
        x_landed = [sem(f"x_landed{i}") for i in range(4)]
        xt_hi_ready = sem("xt_hi_ready")
        xt_lo_ready = sem("xt_lo_ready")
        chan_landed = sem("chan_landed")
        sinks_landed = sem("sinks_landed")
        table_landed = sem("table_landed")
        table_filled = sem("table_filled")
        sinks_ready = sem("sinks_ready")
        soft_step = sem("soft_step")
        soft_exp = sem("soft_exp")
        scales_ready = sem("scales_ready")
        rows_done = sem("rows_done")
        rows_copied = sem("rows_copied")
        rows_stored = sem("rows_stored")
        bias_landed = sem("bias_landed")
        ident_zero = sem("ident_zero")
        ident_ready = sem("ident_ready")
        k_saved = sem("k_saved")
        vt_saved = sem("vt_saved")
        v_turned = sem("v_turned")
        v_saved = sem("v_saved")
        sig_qg_ready = sem("sig_qg_ready")
        qk_staged = sem("qk_staged")
        v_staged = sem("v_staged")
        scores_done = sem("scores_done")
        prev_masked = sem("prev_masked")
        biased = sem("biased")
        row_max = sem("row_max")
        shift_ready = sem("shift_ready")
        sink_shifted = sem("sink_shifted")
        exp_done = sem("exp_done")
        denom_ready = sem("denom_ready")
        recip_ready = sem("recip_ready")
        probs_ready = sem("probs_ready")
        turned = sem("turned")
        turned_saved = sem("turned_saved")
        pv_done = sem("pv_done")
        attn_gated = sem("attn_gated")
        ag_hi_ready = sem("ag_hi_ready")
        ag_lo_ready = sem("ag_lo_ready")
        attn_mixed = sem("attn_mixed")
        gate_w_landed = sem("gate_w_landed")
        conv_begun = sem("conv_begun")
        conv_tap = sem("conv_tap")
        gates_done = sem("gates_done")
        sig_r_ready = sem("sig_r_ready")
        sig_i_ready = sem("sig_i_ready")
        gated_x = sem("gated_x")
        decay_ready = sem("decay_ready")
        tanh_ready = sem("tanh_ready")
        decay_sq = sem("decay_sq")
        norm_sq = sem("norm_sq")
        norm_ready = sem("norm_ready")
        drive_ready = sem("drive_ready")
        scan_done = sem("scan_done")
        sig_gr_ready = sem("sig_gr_ready")
        branch_ready = sem("branch_ready")
        hg_hi_ready = sem("hg_hi_ready")
        hg_lo_ready = sem("hg_lo_ready")
        sig_mr_ready = sem("sig_mr_ready")
        mixed_r_ready = sem("mixed_r_ready")
        merged_ready = sem("merged_ready")
        mg_hi_ready = sem("mg_hi_ready")
        mg_lo_ready = sem("mg_lo_ready")
        ln_landed = sem("ln_landed")
        res_landed = [sem(f"res_landed{s}") for s in range(NB)]
        wo_released = sem("wo_released")
        rows_summed = sem("rows_summed")
        z_ready = sem("z_ready")
        stats_ready = sem("stats_ready")
        mom_ready = sem("mom_ready")
        var_ready = sem("var_ready")
        std_ready = sem("std_ready")
        rstd_ready = sem("rstd_ready")
        centred = sem("centred")
        normed = sem("normed")
        stored = sem("stored")

        block = ctx.enter_context(nc.Block())

        @block.sync
        def _(sp_eng):
            def load_half(turn, half, src):
                if not (isinstance(turn, int) and turn == 0):
                    sp_eng.wait_ge(lo_ready, 4 * turn + 2 * half - 2)
                shape = raw[:, half, :, :]
                if src.shape[1] != 8:
                    shape = shape.rearrange("p (k a) n -> p k (a n)", k=src.shape[1])
                sp_eng.dma_start(shape, src).then_inc(raw_landed[half], 16)

            def load_turn(turn, src_v, col):
                for half in range(2):
                    load_half(turn, half, src_v[:, 8 * half:8 * half + 8, ds(col, P)])

            for u in range(2 * KVT):
                load_turn(T_KV + u, w_in_v, COL_KV + P * u)
            with sp_eng.Fori(0, AT) as j:
                load_turn(T_QG + 2 * j, w_in_v, COL_Q + P * j)
                load_turn(T_QG + 1 + 2 * j, w_in_v, COL_GA + P * j)
            with sp_eng.Fori(0, KT) as c:
                load_turn(T_MA + c, w_in_v, COL_MA + P * c)
            with sp_eng.Fori(0, KT // 2) as c:
                for half in range(2):
                    load_half(T_AO + c, half, w_ao_v[:, :, ds(2 * P * c + P * half, P)])
            with sp_eng.Fori(0, KT) as c:
                load_turn(T_RN + 2 * c, w_in_v, COL_X + P * c)
                load_turn(T_RN + 1 + 2 * c, w_in_v, COL_GR + P * c)
                sp_eng.wait_ge(multiplied, 4 * T_RN + 1 + 8 * c)
                sp_eng.dma_start(gate_w[:, 0:1, :], w_r_v[:, ds(c, 1), :]).then_inc(gate_w_landed, 16)
                sp_eng.dma_start(gate_w[:, 1:2, :], w_i_v[:, ds(c, 1), :]).then_inc(gate_w_landed, 16)
            with sp_eng.Fori(1, KT + 1) as n:
                load_turn(T_MX - 2 + 2 * n, w_in_v, COL_MR - P + P * n)
                load_turn(T_MX - 1 + 2 * n, w_ro_v, P * n - P)
            with sp_eng.Fori(0, 4) as g:
                for h in range(KT // 2):
                    load_half(T_WO + h // 2 + 4 * g, h % 2, w_out_v[:, 2 * h:2 * h + 2, ds(S * g, S)])
            for s in range(NB):
                parts = 4 if s == NB - 1 else 1
                for i in range(parts):
                    n = D // parts
                    sp_eng.wait_ge(normed, 4 * s + 4 * (i + 1) // parts)
                    sp_eng.dma_start(out_v[:, s, i * n:(i + 1) * n],
                                     merged[:, 4 * s:4 * s + 4, :].rearrange("p a n -> p (a n)")[:, i * n:(i + 1) * n]
                                     ).then_inc(stored, 16)
            sp_eng.wait_ge(stored, 16 * (NB + 3))

        @block.gpsimd
        def _(pool):
            nc.gpsimd.memset(ident[:, :], 0.0).then_inc(ident_zero, 1)
            pool.wait_ge(ident_zero, 1)
            nc.gpsimd.affine_select(out=ident[:, :], in_=ident[:, :], compare_op=ALU.not_equal, fill=1.0,
                                    base=0, pattern=[[-1, P]], channel_multiplier=1).then_inc(ident_ready, 1)
            pool.wait_ge(rows_copied, 1)
            pool.dma_start(bias_rows_d, bias_rows[:, :].unsqueeze(1).broadcast_to([HEADS, P, SPAN])
                           ).then_inc(rows_stored, 16)
            pool.wait_ge(rows_stored, 16)
            pool.dma_start(bias[:, :, :], bass.AP(tensor=bias_rows_d.tensor, offset=P - 1,
                                                  ap=[[SPAN - 1, P], [P * SPAN, HEADS], [1, 2 * P]])).then_inc(bias_landed, 16)

            def stage(i, b, g, first_block, first):
                if first:
                    pool.wait_ge(a_free, A_MA)
                    pool.wait_ge(k_saved, 4 * KVT)
                else:
                    pool.wait_ge(scores_done, 2 * i)
                nc.gpsimd.tensor_copy(q_item[:, :], q_sb[:, :, :].rearrange("p b n -> p (b n)")[:, ds(2 * P * i, 2 * P)]
                                      ).then_inc(qk_staged, 1)
                keys = k_sb[:, :, :].rearrange("p g s -> p (g s)")
                if first_block:
                    nc.gpsimd.tensor_copy(k_item[:, 0:P], keys[:, ds(S * g, P)]).then_inc(qk_staged, 1)
                    nc.gpsimd.tensor_copy(k_item[:, P:2 * P], keys[:, ds(S * g, P)]).then_inc(qk_staged, 1)
                else:
                    nc.gpsimd.tensor_copy(k_item[:, :], keys[:, ds(S * g + P * b - P, 2 * P)]).then_inc(qk_staged, 2)
                if first:
                    pool.wait_ge(v_saved, KVT)
                else:
                    pool.wait_ge(pv_done, i)
                values = v_sb[:, :, :].rearrange("p b n -> p (b n)")
                row = KV_HEADS * HD
                last = 0 if first_block else 1
                nc.gpsimd.tensor_copy(v_item[:, 0, :], values[:, ds(row * b + HD * g - row * last, HD)]).then_inc(v_staged, 1)
                nc.gpsimd.tensor_copy(v_item[:, 1, :], values[:, ds(row * b + HD * g, HD)]).then_inc(v_staged, 1)

            stage(0, 0, 0, True, True)
            with pool.Fori(1, KV_HEADS) as g:
                stage(g, 0, g, True, False)
            with pool.Fori(1, NB) as b:
                with pool.Fori(0, KV_HEADS) as g:
                    stage(4 * b + g, b, g, False, False)

            pool.wait_ge(hg_lo_ready, KT)
            pool.dma_start(ln_gb[:, 0, :], ln_g.partition_broadcast(P)).then_inc(ln_landed, 16)
            pool.dma_start(ln_gb[:, 1, :], ln_b.partition_broadcast(P)).then_inc(ln_landed, 16)
            pool.wait_ge(mg_lo_ready, KT)
            for s in range(NB):
                pool.dma_start(merged[:, 4 * s:4 * s + 4, :].rearrange("p a n -> p (a n)"), x_v[:, s, :]
                               ).then_inc(res_landed[s], 16)

        @block.scalar
        def _(act):
            for i in range(4):
                a, b = X_CUTS[i], X_CUTS[i + 1]
                act.dma_start(merged[:, a:b, :], x_t_v[:, a:b, :]).then_inc(x_landed[i], 16)
            act.dma_start(chan_sb[:, :, :], chan).then_inc(chan_landed, 16)
            act.dma_start(sinks_sb[:, :], sinks[0].partition_broadcast(P)).then_inc(sinks_landed, 16)
            act.dma_start(table_sb[:, :], rel_bias).then_inc(table_landed, 16)
            act.dma_start(buckets[:, :], bucket_rows).then_inc(table_landed, 16)

            def high_parts(turn, quarters):
                for s in quarters:
                    if s % 2 == 0:
                        act.wait_ge(raw_landed[s // 2], 16 * turn + 16)
                    if not (isinstance(turn, int) and turn == 0):
                        act.wait_ge(multiplied, 4 * turn + s - 3)
                    nc.scalar.activation(w_hi[:, s, :, :], raw[:, s // 2, 4 * (s % 2):4 * (s % 2) + 4, :], ACT.Copy
                                         ).then_inc(hi_ready, 1)

            def high_chunk(g, k):
                turn, s = T_WO + k // 4 + 4 * g, k % 4
                if s % 2 == 0:
                    act.wait_ge(raw_landed[s // 2], 16 * turn + 16)
                if isinstance(g, int) and g == 0:
                    act.wait_ge(multiplied, 4 * T_WO)
                else:
                    act.wait_ge(wo_released, KT * g - KT + k + 1)
                nc.scalar.activation(hg_hi[:, k, :], raw[:, s // 2, 4 * (s % 2):4 * (s % 2) + 4, :].rearrange("p k n -> p (k n)"),
                                     ACT.Copy).then_inc(hi_ready, 1)

            for i in range(4):
                act.wait_ge(x_landed[i], 16)
                if i == 0:
                    high_parts(0, [0])
                for k in range(X_CUTS[i], X_CUTS[i + 1]):
                    nc.scalar.activation(xt_hi[:, k, :], merged[:, k, :], ACT.Copy).then_inc(xt_hi_ready, 1)
                    if k in (3, 7, 11):
                        high_parts(0, [(k + 1) // 4])
            act.wait_ge(soft_step, 2)
            nc.scalar.activation(sp[:, 1, :], sp[:, 1, :], ACT.Exp).then_inc(soft_exp, 1)
            for u in range(2 * KVT):
                high_parts(T_KV + u + 1, range(4))

            with act.Fori(0, AT) as j:
                high_parts(T_QG + 1 + 2 * j, range(4))
                high_parts(T_QG + 2 + 2 * j, range(4))
                act.wait_ge(multiplied, 4 * T_QG + 8 + 8 * j)
                nc.scalar.activation(sig_qg[:, :], bank_b[:, :], ACT.Sigmoid).then_inc(sig_qg_ready, 1)

            def attention_item(i):
                act.wait_ge(sink_shifted, i + 1)
                nc.scalar.activation(small[:, 3, :], small[:, 2, :], ACT.Exp).then_inc(exp_done, 1)
                for h in range(GROUP):
                    nc.scalar.activation(probs[:, h, :], probs[:, h, :], ACT.Exp, bias=small[:, 1, h:h + 1],
                                         accum_out=small[:, 4, h:h + 1]).then_inc(exp_done, 1)
                high_parts(T_MA + 1 + i, range(4))
                act.wait_ge(multiplied, 4 * T_MA + 4 + 4 * i)
                nc.scalar.activation(merged[:, ds(i, 1), :], bank_a[:, :].unsqueeze(1), ACT.Sigmoid).then_inc(a_free, 1)

            with act.Fori(0, ITEMS) as i:
                attention_item(i)

            for k in range(AT):
                act.wait_ge(attn_gated, ITEMS if k >= AT - 2 else ITEMS - 1)
                nc.scalar.activation(ag_hi[:, k, :].rearrange("p (b n) -> p b n", b=NB),
                                     g_attn[:, :, k * P:(k + 1) * P], ACT.Copy).then_inc(ag_hi_ready, 1)
            with act.Fori(0, KT // 2) as c:
                high_parts(T_AO + 1 + c, range(4))

            def gate_sigmoids(c):
                act.wait_ge(gates_done, c + 1)
                nc.scalar.activation(rec_gate[:, :], bank_s[:, 0, :], ACT.Sigmoid, bias=chan_sb[:, ds(c, 1), 5]
                                     ).then_inc(sig_r_ready, 1)
                nc.scalar.activation(inp[:, :], bank_s[:, 1, :], ACT.Sigmoid, bias=chan_sb[:, ds(c, 1), 6]
                                     ).then_inc(sig_i_ready, 1)

            def decays(c):
                act.wait_ge(sig_r_ready, c + 1)
                nc.scalar.activation(decay[:, :], rec_gate[:, :], ACT.Exp, scale=exp_scale[:, ds(c, 1)]
                                     ).then_inc(decay_ready, 1)
                nc.scalar.activation(norm[:, :], rec_gate[:, :], ACT.Tanh, scale=tanh_scale[:, ds(c, 1)]
                                     ).then_inc(tanh_ready, 1)

            def norm_root(c):
                act.wait_ge(norm_sq, c + 1)
                nc.scalar.activation(norm[:, :], norm[:, :], ACT.Sqrt).then_inc(norm_ready, 1)

            def branch_high(c):
                act.wait_ge(branch_ready, c + 1)
                nc.scalar.activation(hg_hi[:, ds(c, 1), :], gated[:, :].unsqueeze(1), ACT.Copy).then_inc(hg_hi_ready, 1)

            def recurrent_tile(c, first):
                if not first:
                    gate_sigmoids(c - 1)
                high_parts(T_RN + 1 + 2 * c, [0])
                if not first:
                    decays(c - 1)
                high_parts(T_RN + 1 + 2 * c, [1, 2])
                if not first:
                    norm_root(c - 1)
                high_parts(T_RN + 1 + 2 * c, [3])
                act.wait_ge(multiplied, 4 * T_RN + 4 + 8 * c)
                if not first:
                    act.wait_ge(gated_x, c)
                nc.scalar.activation(xc[:, :], bank_a[:, :], ACT.Identity, scale=chan_sb[:, ds(c, 1), 3],
                                     bias=chan_sb[:, ds(c, 1), 4]).then_inc(conv_begun, 1)
                high_parts(T_RN + 2 + 2 * c, [0, 1])
                if not first:
                    branch_high(c - 1)
                high_parts(T_RN + 2 + 2 * c, [2, 3])
                act.wait_ge(multiplied, 4 * T_RN + 8 + 8 * c)
                nc.scalar.activation(silu[:, :], bank_b[:, :], ACT.Sigmoid).then_inc(sig_gr_ready, 1)

            recurrent_tile(0, True)
            with act.Fori(1, KT) as c:
                recurrent_tile(c, False)

            def merge_tile(c, first=False, last=False):
                if first:
                    gate_sigmoids(KT - 1)
                high_parts(T_MX + 1 + 2 * c, [0])
                if first:
                    decays(KT - 1)
                high_parts(T_MX + 1 + 2 * c, [1, 2])
                if first:
                    norm_root(KT - 1)
                high_parts(T_MX + 1 + 2 * c, [3])
                if first:
                    branch_high(KT - 1)
                else:
                    act.wait_ge(mixed_r_ready, c)
                act.wait_ge(multiplied, 4 * T_MX + 4 + 8 * c)
                nc.scalar.activation(sig_mr[:, :], bank_a[:, :], ACT.Sigmoid).then_inc(sig_mr_ready, 1)
                if not last:
                    high_parts(T_MX + 2 + 2 * c, range(4))

            merge_tile(0, first=True)
            with act.Fori(1, KT - 1) as c:
                merge_tile(c)
            merge_tile(KT - 1, last=True)

            for k in range(KT):
                act.wait_ge(merged_ready, k + 1)
                nc.scalar.activation(xt_hi[:, k, :], merged[:, k, :], ACT.Copy).then_inc(mg_hi_ready, 1)
                if k == KT - 1:
                    for kk in range(1, KT):
                        high_chunk(0, kk)
                elif k == KT - 2:
                    high_chunk(0, 0)
            with act.Fori(1, 4) as g:
                for k in range(KT):
                    high_chunk(g, k)
            for s in range(NB):
                act.wait_ge(var_ready, s + 1)
                nc.scalar.activation(spread[:, s, 0:1], moments[:, s, 1:2], ACT.Sqrt).then_inc(std_ready, 1)

        @block.vector
        def _(dve):
            V = nc.vector

            def low_parts(turn, quarters):
                for s in quarters:
                    dve.wait_ge(hi_ready, 4 * turn + s + 1)
                    V.tensor_tensor(w_lo[:, s, :, :], raw[:, s // 2, 4 * (s % 2):4 * (s % 2) + 4, :],
                                    w_hi[:, s, :, :], ALU.subtract).then_inc(lo_ready, 1)

            def low_chunk(g, k):
                s = k % 4
                dve.wait_ge(hi_ready, 4 * T_WO + KT * g + k + 1)
                V.tensor_tensor(hg_lo[:, k, :], raw[:, s // 2, 4 * (s % 2):4 * (s % 2) + 4, :].rearrange("p k n -> p (k n)"),
                                hg_hi[:, k, :], ALU.subtract).then_inc(lo_ready, 1)

            V.memset(bias_table[BUCKETS:BUCKETS + 1, :], NEG_INF).then_inc(table_filled, 1)
            low_parts(0, [0])
            for k in range(KT):
                dve.wait_ge(xt_hi_ready, k + 1)
                V.tensor_tensor(xt_lo[:, k, :], merged[:, k, :], xt_hi[:, k, :], ALU.subtract).then_inc(xt_lo_ready, 1)
                if k in (3, 7, 11):
                    low_parts(0, [(k + 1) // 4])

            steps = 0

            def then_next(ins):
                nonlocal steps
                steps += 1
                ins.then_inc(soft_step, 1)
                dve.wait_ge(soft_step, steps)

            lam, negated, e, z, z2, acc = chan_sb[:, :, 7], sp[:, 0, :], sp[:, 1, :], sp[:, 2, :], sp[:, 3, :], sp[:, 4, :]
            dve.wait_ge(chan_landed, 16)
            then_next(V.tensor_scalar(negated, lam, -1.0, None, ALU.mult))
            then_next(V.tensor_tensor(e, negated, lam, ALU.min))
            dve.wait_ge(soft_exp, 1)
            then_next(V.tensor_scalar(z, e, 2.0, None, ALU.add))
            then_next(V.reciprocal(acc, z))
            then_next(V.tensor_tensor(z, e, acc, ALU.mult))
            then_next(V.tensor_tensor(z2, z, z, ALU.mult))
            then_next(V.tensor_scalar(acc, z2, 1.0 / 17, None, ALU.mult))
            for n in (15, 13, 11, 9, 7, 5, 3):
                then_next(V.scalar_tensor_tensor(acc, acc, 1.0 / n, z2, ALU.add, ALU.mult))
            then_next(V.scalar_tensor_tensor(acc, acc, 1.0, z, ALU.add, ALU.mult))
            then_next(V.tensor_scalar(negated, negated, 0.0, None, ALU.max))
            then_next(V.scalar_tensor_tensor(acc, acc, 2.0, negated, ALU.mult, ALU.add))
            V.tensor_scalar(exp_scale[:, :], acc, -LRU_C, None, ALU.mult).then_inc(scales_ready, 1)
            V.tensor_scalar(tanh_scale[:, :], acc, LRU_C, None, ALU.mult).then_inc(scales_ready, 1)
            dve.wait_ge(sinks_landed, 16)
            V.tensor_scalar(neg_sinks[:, :].rearrange("p (g h t) -> p g h t", t=2, h=2),
                            sinks_sb[:, :].rearrange("p (g t h) -> p g h t", t=2, h=2), -1.0, None, ALU.mult).then_inc(sinks_ready, 1)

            dve.wait_ge(table_landed, 32)
            V.tensor_copy(bias_table[0:BUCKETS, :].rearrange("p (g h t) -> p g h t", t=2, h=2),
                          table_sb[:, :].rearrange("p (g t h) -> p g h t", t=2, h=2)).then_inc(table_filled, 1)

            for u in range(2 * KVT):
                low_parts(T_KV + u + 1, range(4))
                dve.wait_ge(multiplied, 4 * (T_KV + u + 1))
                bank, free = (bank_a, a_free) if u % 2 == 0 else (bank_b, b_free)
                if u < KVT:
                    for head in range(2):
                        for half in range(2):
                            V.tensor_copy(k_sb[64 * half:64 * half + 64, 2 * u + head, :],
                                                bank[64 * head:64 * head + 64, :]).then_inc(k_saved, 1)
                    dve.wait_ge(k_saved, 4 * (u + 1))
                    dve.sem_inc(free, 1)
                else:
                    V.tensor_copy(v_t[:, u - KVT, :], bank[:, :]).then_inc(free, 1)
                if u == 0:
                    dve.wait_ge(rows_done, 1)
                    V.tensor_copy(bias_rows[:, :], bank_o[0:HEADS, 0:SPAN]).then_inc(rows_copied, 1)

            with dve.Fori(0, AT) as j:
                low_parts(T_QG + 1 + 2 * j, range(4))
                dve.wait_ge(multiplied, 4 * T_QG + 4 + 8 * j)
                V.tensor_copy(q_sb[:, :, ds(P * j, P)], bank_a[:, :].rearrange("p (b n) -> p b n", b=NB)
                              ).then_inc(a_free, 1)
                low_parts(T_QG + 2 + 2 * j, range(4))
                dve.wait_ge(sig_qg_ready, j + 1)
                V.tensor_tensor(g_attn[:, :, ds(P * j, P)], bank_b[:, :].rearrange("p (b n) -> p b n", b=NB),
                                sig_qg[:, :].rearrange("p (b n) -> p b n", b=NB), ALU.mult).then_inc(b_free, 1)
            for t in range(KVT):
                dve.wait_ge(v_turned, t + 1)
                V.tensor_copy(v_sb[:, :, t * P:(t + 1) * P], bank_t[:, t, :].rearrange("p (b n) -> p b n", b=NB)
                              ).then_inc(v_saved, 1)

            def gate_item(i):
                dve.wait_ge(pv_done, i + 1)
                place = g_attn[:, :, :].rearrange("p b n -> p (b n)")[:, ds(2 * P * i, 2 * P)]
                V.tensor_tensor(place, bank_o[:, 0:2 * P], place, ALU.mult).then_inc(attn_gated, 1)

            def attention_item(i, g, first_block, first):
                dve.wait_ge(scores_done, 2 * i + 2)
                if first_block:
                    V.memset(probs[:, :, 0:P], NEG_INF).then_inc(prev_masked, 1)
                    V.scalar_tensor_tensor(probs[:, :, P:2 * P], scores[:, :, P:2 * P], SCALE,
                                           bias[:, ds(GROUP * g, GROUP), P:2 * P], ALU.mult, ALU.add).then_inc(biased, 1)
                    dve.wait_ge(prev_masked, i + 1)
                else:
                    V.scalar_tensor_tensor(probs[:, :, :], scores, SCALE, bias[:, ds(GROUP * g, GROUP), :],
                                           ALU.mult, ALU.add).then_inc(biased, 1)
                dve.wait_ge(biased, i + 1)
                V.tensor_reduce(small[:, 0, :], probs[:, :, :], AX.X, ALU.max).then_inc(row_max, 1)
                dve.wait_ge(row_max, i + 1)
                V.scalar_tensor_tensor(small[:, 1, :], small[:, 0, :], -1.0, neg_sinks[:, ds(GROUP * g, GROUP)],
                                       ALU.mult, ALU.min).then_inc(shift_ready, 1)
                dve.wait_ge(shift_ready, i + 1)
                V.tensor_tensor(small[:, 2, :], small[:, 1, :], neg_sinks[:, ds(GROUP * g, GROUP)], ALU.subtract
                                ).then_inc(sink_shifted, 1)
                if not first:
                    gate_item(i - 1)
                low_parts(T_MA + 1 + i, [0, 1])
                dve.wait_ge(exp_done, 5 * i + 5)
                V.tensor_tensor(small[:, 4, :], small[:, 4, :], small[:, 3, :], ALU.add).then_inc(denom_ready, 1)
                dve.wait_ge(denom_ready, i + 1)
                V.reciprocal(small[:, 5, :], small[:, 4, :]).then_inc(recip_ready, 1)
                dve.wait_ge(recip_ready, i + 1)
                V.tensor_tensor(probs[:, :, :], probs[:, :, :],
                                small[:, 5, :].unsqueeze(2).broadcast_to([P, GROUP, 2 * P]), ALU.mult
                                ).then_inc(probs_ready, 1)
                low_parts(T_MA + 1 + i, [2, 3])
                dve.wait_ge(turned, i + 1)
                for w in range(2):
                    V.tensor_copy(probs_t[:, w, :], bank_t[:, w, :]).then_inc(turned_saved, 1)

            dve.wait_ge(bias_landed, 16)
            dve.wait_ge(sinks_ready, 1)
            attention_item(0, 0, True, True)
            with dve.Fori(1, KV_HEADS) as g:
                attention_item(g, g, True, False)
            with dve.Fori(1, NB) as b:
                with dve.Fori(0, KV_HEADS) as g:
                    attention_item(4 * b + g, g, False, False)
            gate_item(ITEMS - 1)

            for k in range(AT):
                dve.wait_ge(ag_hi_ready, k + 1)
                V.tensor_tensor(ag_lo[:, k, :].rearrange("p (b n) -> p b n", b=NB), g_attn[:, :, k * P:(k + 1) * P],
                                ag_hi[:, k, :].rearrange("p (b n) -> p b n", b=NB), ALU.subtract).then_inc(ag_lo_ready, 1)
            dve.wait_ge(a_free, A_AO)
            with dve.Fori(0, KT // 2) as c:
                for bank, free, half in ((bank_a, a_free, 0), (bank_b, b_free, 1)):
                    low_parts(T_AO + 1 + c, [2 * half, 2 * half + 1])
                    dve.wait_ge(multiplied, 4 * T_AO + 2 + 2 * half + 4 * c)
                    V.tensor_tensor(merged[:, ds(2 * c + half, 1), :], bank[:, :].unsqueeze(1),
                                    merged[:, ds(2 * c + half, 1), :], ALU.mult).then_inc(free, 1)

            def drive_input(c):
                dve.wait_ge(sig_i_ready, c + 1)
                V.tensor_tensor(inp[:, :], inp[:, :], xc[:, :], ALU.mult).then_inc(gated_x, 1)

            def norm_square(c):
                dve.wait_ge(decay_ready, c + 1)
                V.tensor_tensor(hid[:, :], decay[:, :], decay[:, :], ALU.mult).then_inc(decay_sq, 1)
                dve.wait_ge(decay_sq, c + 1)
                dve.wait_ge(tanh_ready, c + 1)
                V.scalar_tensor_tensor(norm[:, :], hid[:, :], 1.0, norm[:, :], ALU.add, ALU.mult).then_inc(norm_sq, 1)

            def recurrence(c):
                dve.wait_ge(norm_ready, c + 1)
                dve.wait_ge(gated_x, c + 1)
                V.tensor_tensor(inp[:, :], inp[:, :], norm[:, :], ALU.mult).then_inc(drive_ready, 1)
                dve.wait_ge(drive_ready, c + 1)
                V.tensor_tensor_scan(hid[:, :], decay[:, :], inp[:, :], 0.0, ALU.mult, ALU.add).then_inc(scan_done, 1)
                dve.wait_ge(scan_done, c + 1)
                dve.wait_ge(b_free, B_RN + 1 + c)
                V.tensor_tensor(gated[:, :], hid[:, :], silu[:, :], ALU.mult).then_inc(branch_ready, 1)

            def branch_low(c):
                dve.wait_ge(hg_hi_ready, c + 1)
                V.tensor_tensor(hg_lo[:, ds(c, 1), :], gated[:, :].unsqueeze(1), hg_hi[:, ds(c, 1), :], ALU.subtract
                                ).then_inc(hg_lo_ready, 1)

            def recurrent_tile(c, first):
                if not first:
                    drive_input(c - 1)
                low_parts(T_RN + 1 + 2 * c, [0, 1])
                if not first:
                    norm_square(c - 1)
                low_parts(T_RN + 1 + 2 * c, [2, 3])
                dve.wait_ge(conv_begun, c + 1)
                for tap in range(3):
                    back = tap + 1
                    if tap:
                        dve.wait_ge(conv_tap, 3 * c + tap)
                    V.scalar_tensor_tensor(xc[:, back:S], bank_a[:, 0:S - back], chan_sb[:, ds(c, 1), 3 - back],
                                                 xc[:, back:S], ALU.mult, ALU.add).then_inc(conv_tap, 1)
                dve.wait_ge(conv_tap, 3 * c + 3)
                dve.sem_inc(a_free, 1)
                low_parts(T_RN + 2 + 2 * c, [0])
                if not first:
                    recurrence(c - 1)
                low_parts(T_RN + 2 + 2 * c, [1])
                if not first:
                    branch_low(c - 1)
                low_parts(T_RN + 2 + 2 * c, [2, 3])
                dve.wait_ge(sig_gr_ready, c + 1)
                V.tensor_tensor(silu[:, :], bank_b[:, :], silu[:, :], ALU.mult).then_inc(b_free, 1)

            recurrent_tile(0, True)
            with dve.Fori(1, KT) as c:
                recurrent_tile(c, False)

            def merge_tile(c, first=False, last=False):
                if first:
                    drive_input(KT - 1)
                low_parts(T_MX + 1 + 2 * c, [0, 1])
                if first:
                    norm_square(KT - 1)
                low_parts(T_MX + 1 + 2 * c, [2, 3])
                if first:
                    recurrence(KT - 1)
                    branch_low(KT - 1)
                if not last:
                    low_parts(T_MX + 2 + 2 * c, range(4))
                else:
                    for k in range(KT - 1):
                        dve.wait_ge(mg_hi_ready, k + 1)
                        V.tensor_tensor(xt_lo[:, k, :], merged[:, k, :], xt_hi[:, k, :], ALU.subtract
                                        ).then_inc(mg_lo_ready, 1)
                dve.wait_ge(sig_mr_ready, c + 1)
                dve.wait_ge(multiplied, 4 * T_MX + 8 + 8 * c)
                V.tensor_tensor(mixed_r[:, :], bank_b[:, :], sig_mr[:, :], ALU.mult).then_inc(mixed_r_ready, 1)
                dve.wait_ge(mixed_r_ready, c + 1)
                V.tensor_tensor(merged[:, ds(c, 1), :], merged[:, ds(c, 1), :], mixed_r[:, :].unsqueeze(1), ALU.add
                                ).then_inc(merged_ready, 1)

            merge_tile(0, first=True)
            with dve.Fori(1, KT - 1) as c:
                merge_tile(c)
            merge_tile(KT - 1, last=True)
            low_chunk(0, 0)
            dve.wait_ge(mg_hi_ready, KT)
            V.tensor_tensor(xt_lo[:, KT - 1, :], merged[:, KT - 1, :], xt_hi[:, KT - 1, :], ALU.subtract
                            ).then_inc(mg_lo_ready, 1)
            for k in range(1, KT):
                low_chunk(0, k)

            z_rows = [merged[:, 4 * s:4 * s + 4, :] for s in range(NB)]

            def add_residual(g, s):
                if isinstance(g, int) and g == 0:
                    dve.wait_ge(res_landed[s], 16)
                dve.wait_ge(rows_summed, NB * g + s + 1)
                z = merged[:, ds(4 * s + g, 1), :]
                V.scalar_tensor_tensor(z, z, ALPHA, out_banks[s].unsqueeze(1), ALU.mult, ALU.add).then_inc(z_ready, 1)
                dve.wait_ge(z_ready, NB * g + s + 1)
                V.bn_stats(stats[:, s, ds(g, 1), :].rearrange("p a n -> p (a n)"), z.rearrange("p a n -> p (a n)")
                           ).then_inc(stats_ready, 1)

            def normalise(s):
                dve.wait_ge(stats_ready, NB * 3 + s + 1)
                V.bn_aggr(moments[:, s, :], stats[:, s, :, :].rearrange("p a n -> p (a n)")).then_inc(mom_ready, 1)
                dve.wait_ge(mom_ready, s + 1)
                V.tensor_scalar(moments[:, s, 1:2], moments[:, s, 1:2], LN_EPS, None, ALU.add).then_inc(var_ready, 1)
                dve.wait_ge(std_ready, s + 1)
                V.reciprocal(spread[:, s, 1:2], spread[:, s, 0:1]).then_inc(rstd_ready, 1)
                dve.wait_ge(rstd_ready, s + 1)
                for i in range(4):
                    z = z_rows[s][:, i, :]
                    V.scalar_tensor_tensor(z, z, moments[:, s, 0:1], ln_gb[:, 0, i * S:(i + 1) * S], ALU.subtract,
                                           ALU.mult).then_inc(centred, 1)
                    dve.wait_ge(centred, 4 * s + i + 1)
                    V.scalar_tensor_tensor(z, z, spread[:, s, 1:2], ln_gb[:, 1, i * S:(i + 1) * S], ALU.mult, ALU.add
                                           ).then_inc(normed, 1)

            def column_group(g):
                for s in range(NB - 1):
                    add_residual(g, s)
                for k in range(KT):
                    low_chunk(g + 1, k)
                add_residual(g, NB - 1)

            column_group(0)
            with dve.Fori(1, 3) as g:
                column_group(g)
            dve.wait_ge(ln_landed, 32)
            for s in range(NB):
                add_residual(3, s)
                normalise(s)

        @block.tensor
        def _(pe):
            mm = nc.tensor.matmul

            def multiply(turn, quarters, act_hi, act_lo, bank, k_tiles=KT, before_tile=None):
                for s in quarters:
                    pe.wait_ge(lo_ready, 4 * turn + s + 1)
                    for kk in range(4):
                        k = (4 * s + kk) % k_tiles
                        if before_tile:
                            before_tile(k)
                        mm(bank, w_hi[:, s, kk, :], act_hi[:, k, :], start=(k == 0), stop=False)
                        mm(bank, w_hi[:, s, kk, :], act_lo[:, k, :], start=False, stop=False)
                        last = mm(bank, w_lo[:, s, kk, :], act_hi[:, k, :], start=False, stop=(k == k_tiles - 1))
                    last.then_inc(multiplied, 1)

            def x_tile_ready(k):
                pe.wait_ge(xt_lo_ready, k + 1)

            for u in range(2 * KVT):
                if u >= 2:
                    pe.wait_ge((a_free, b_free)[u % 2], u // 2)
                multiply(T_KV + u, range(4), xt_hi, xt_lo, (bank_a, bank_b)[u % 2][:, :],
                         before_tile=x_tile_ready if u == 0 else None)
                if u == 0:
                    pe.wait_ge(table_landed, 32)
                    pe.wait_ge(table_filled, 2)
                    mm(bank_o[0:HEADS, 0:SPAN], bias_table[:, :], buckets[:, :], start=True, stop=True
                       ).then_inc(rows_done, 1)

            with pe.Fori(0, AT) as j:
                pe.wait_ge(a_free, A_QG + j)
                multiply(T_QG + 2 * j, range(4), xt_hi, xt_lo, bank_a[:, :])
                pe.wait_ge(b_free, B_QG + j)
                multiply(T_QG + 1 + 2 * j, range(4), xt_hi, xt_lo, bank_b[:, :])
            pe.wait_ge(ident_ready, 1)
            pe.wait_ge(b_free, KVT)
            for t in range(KVT):
                for b in range(NB):
                    ins = nc.tensor.transpose(bank_t[:, t, b * P:(b + 1) * P], v_t[:, t, b * P:(b + 1) * P], ident[:, :])
                ins.then_inc(v_turned, 1)

            def score(i, first):
                pe.wait_ge(qk_staged, 3 * i + 3)
                if not first:
                    pe.wait_ge(biased, i)
                for t in range(2):
                    for half in range(2):
                        rows = slice(64 * half, 64 * half + 64)
                        ins = mm(scores[:, 2 * half + t, :], q_item[rows, t * P:(t + 1) * P], k_item[rows, :],
                                 start=True, stop=True)
                        if t == 1:
                            ins.then_inc(scores_done, 1)

            def weigh_values(i, first):
                pe.wait_ge(turned_saved, 2 * i + 2)
                pe.wait_ge(v_staged, 2 * i + 2)
                if not first:
                    pe.wait_ge(attn_gated, i)
                for half in range(2):
                    for w in range(2):
                        ins = mm(bank_o[64 * half:64 * half + 64, 0:2 * P], v_item[:, w, :],
                                 probs_t[:, w, 2 * P * half:2 * P * half + 2 * P],
                                 start=(w == 0), stop=(w == 1))
                ins.then_inc(pv_done, 1)

            def turn_probs(i):
                pe.wait_ge(probs_ready, i + 1)
                for w in range(2):
                    for h in range(GROUP):
                        ins = nc.tensor.transpose(bank_t[:, w, h * P:(h + 1) * P], probs[:, h, w * P:(w + 1) * P],
                                                  ident[:, :])
                ins.then_inc(turned, 1)

            pe.wait_ge(v_saved, KVT)
            score(0, True)
            pe.wait_ge(a_free, A_MA)
            multiply(T_MA, range(4), xt_hi, xt_lo, bank_a[:, :])
            turn_probs(0)
            score(1, False)
            weigh_values(0, True)
            pe.wait_ge(a_free, A_MA + 1)
            multiply(T_MA + 1, range(4), xt_hi, xt_lo, bank_a[:, :])
            turn_probs(1)
            with pe.Fori(2, ITEMS) as i:
                score(i, False)
                weigh_values(i - 1, False)
                pe.wait_ge(a_free, A_MA + i)
                multiply(T_MA + i, range(4), xt_hi, xt_lo, bank_a[:, :])
                turn_probs(i)
            weigh_values(ITEMS - 1, False)

            pe.wait_ge(ag_lo_ready, AT)
            with pe.Fori(0, KT // 2) as c:
                pe.wait_ge(a_free, A_AO + c)
                multiply(T_AO + c, [0, 1], ag_hi, ag_lo, bank_a[:, :], k_tiles=AT)
                pe.wait_ge(b_free, B_AO + c)
                multiply(T_AO + c, [2, 3], ag_hi, ag_lo, bank_b[:, :], k_tiles=AT)

            with pe.Fori(0, KT) as c:
                pe.wait_ge(a_free, A_RN + c)
                multiply(T_RN + 2 * c, range(4), xt_hi, xt_lo, bank_a[:, :])
                pe.wait_ge(b_free, B_RN + c)
                multiply(T_RN + 1 + 2 * c, range(4), xt_hi, xt_lo, bank_b[:, :])
                pe.wait_ge(gate_w_landed, 32 * c + 32)
                pe.wait_ge(conv_tap, 3 * c + 3)
                for n in range(2):
                    ins = mm(bank_s[:, n, :], gate_w[:, n, :], xc[:, :], start=True, stop=True)
                ins.then_inc(gates_done, 1)

            pe.wait_ge(a_free, A_MX)
            multiply(T_MX, range(4), xt_hi, xt_lo, bank_a[:, :])
            pe.wait_ge(b_free, B_MX)
            pe.wait_ge(hg_lo_ready, KT)
            multiply(T_MX + 1, range(4), hg_hi, hg_lo, bank_b[:, :])
            with pe.Fori(1, KT) as c:
                pe.wait_ge(sig_mr_ready, c)
                multiply(T_MX + 2 * c, range(4), xt_hi, xt_lo, bank_a[:, :])
                pe.wait_ge(mixed_r_ready, c)
                multiply(T_MX + 1 + 2 * c, range(4), hg_hi, hg_lo, bank_b[:, :])

            def column_group(g, first):
                for s in range(NB):
                    if not first:
                        pe.wait_ge(z_ready, NB * g - NB + s + 1)
                    for k in range(KT):
                        if s == 0:
                            pe.wait_ge(lo_ready, 4 * T_WO + KT * g + k + 1)
                            if first:
                                pe.wait_ge(mg_lo_ready, k + 1)
                        rows = slice(s * P, (s + 1) * P)
                        mm(out_banks[s], xt_hi[:, k, rows], hg_hi[:, k, :], start=(k == 0), stop=False)
                        mm(out_banks[s], xt_lo[:, k, rows], hg_hi[:, k, :], start=False, stop=False)
                        last = mm(out_banks[s], xt_hi[:, k, rows], hg_lo[:, k, :], start=False, stop=(k == KT - 1))
                        if s == NB - 1:
                            last.then_inc(wo_released, 1)
                    if s < NB - 1:
                        last.then_inc(rows_summed, 1)
                    else:
                        pe.wait_ge(wo_released, KT * g + KT)
                        pe.sem_inc(rows_summed, 1)

            column_group(0, True)
            with pe.Fori(1, 4) as g:
                column_group(g, False)


def bucket_row_constants():
    import math

    import numpy as np

    buckets, max_distance, window = 32, 128, 128
    exact = buckets // 2
    rows = np.zeros((buckets + 1, 3 * window), np.float32)
    for t in range(3 * window):
        n = 2 * window - 1 - t
        if not 0 <= n < window:
            b = buckets
        elif n < exact:
            b = n
        else:
            b = min(exact + int(math.log(n / exact) / math.log(max_distance / exact) * (buckets - exact)), buckets - 1)
        rows[b, t] = 1.0
    return rows


def kernel(x, w_in, conv_w, conv_b, w_r, b_r, w_i, b_i, lru_lambda, sinks, w_attn_out, w_rnn_out, w_out,
           ln_g, ln_b, rel_bias):
    import numpy as np
    import concourse.bacc as bacc
    from concourse.bass_utils import run_bass_kernel_spmd

    c = np.ascontiguousarray
    chan = np.concatenate([np.asarray(conv_w)[0], np.asarray(conv_b), np.asarray(b_r), np.asarray(b_i),
                           np.asarray(lru_lambda)])
    chan = c(chan.reshape(8, -1, P).transpose(2, 1, 0))
    arrays = {
        "x_t": c(np.asarray(x)[0].T), "x": c(x), "w_in": c(w_in), "chan": chan, "w_r": c(w_r), "w_i": c(w_i),
        "sinks": c(sinks), "w_attn_out": c(w_attn_out), "w_rnn_out": c(w_rnn_out), "w_out": c(w_out),
        "ln_g": c(ln_g), "ln_b": c(ln_b), "rel_bias": c(rel_bias), "bucket_rows": bucket_row_constants(),
    }
    nc = bacc.Bacc("TRN2", target_bir_lowering=False, num_devices=1)
    args = [nc.dram_tensor(name, a.shape, mybir.dt.from_np(a.dtype), kind="ExternalInput").ap()
            for name, a in arrays.items()]
    out = nc.dram_tensor("out", tuple(np.asarray(x).shape), F32, kind="ExternalOutput").ap()
    hybrid_layer(nc, *args, out)
    r = run_bass_kernel_spmd(nc, [arrays], core_ids=[0])
    return r.results[0]["out"]
```

```python
from contextlib import ExitStack

import concourse.bass as bass
from concourse import mybir

F32 = mybir.dt.float32
F32R = mybir.dt.float32r
ALU = mybir.AluOpType
ACT = mybir.ActivationFunctionType
AX = mybir.AxisListType

P = 128
NEG_INF = -1e30
LN_EPS = 1e-5
LRU_C = 8.0
DEPTH = 1
ALPHA = (2.0 * DEPTH) ** 0.25


def hybrid_layer(nc, x_t, x, w_in, chan, w_r, w_i, sinks, w_attn_out, w_rnn_out, w_out,
                 ln_g, ln_b, rel_bias, bucket_rows, out):
    D, S = x_t.shape
    KT = D // P
    HEADS = sinks.shape[1]
    HD = w_attn_out.shape[1] // HEADS
    KV_HEADS = 4
    GROUP = HEADS // KV_HEADS
    NB = S // P
    AT = HEADS * HD // P
    KVT = KV_HEADS * HD // P
    ITEMS = NB * KV_HEADS
    assert GROUP == 4 and HD == 64 and S == 512 and KT == 16 and ITEMS == KT
    SCALE = HD ** -0.5
    BUCKETS = rel_bias.shape[0]
    SPAN = bucket_rows.shape[1]

    COL_Q = 0
    COL_K = COL_Q + AT * P
    COL_V = COL_K + KVT * P
    COL_GA = COL_V + KVT * P
    COL_X = COL_GA + AT * P
    COL_GR = COL_X + D
    COL_MA = COL_GR + D
    COL_MR = COL_MA + D

    T_VK = 0
    T_QG = T_VK + 2 * KVT
    T_MA = T_QG + 2 * AT
    T_X0 = T_MA + KT
    T_AO = T_X0 + 1
    T_RN = T_AO + KT // 2
    T_MX = T_RN + 2 * KT - 1
    T_WO = T_MX + 2 * KT
    A_QG = KVT
    A_MA = A_QG + AT
    A_AO = A_MA + KT
    A_RN = A_AO + KT // 2
    A_MX = A_RN + KT - 1
    B_QG = KVT
    B_AO = B_QG + AT
    B_RN = B_AO + KT // 2
    B_MX = B_RN + KT

    w_in_v = w_in[0].rearrange("(k p) n -> p k n", p=P)
    w_ao_v = w_attn_out[0].rearrange("(k p) n -> p k n", p=P)
    w_ro_v = w_rnn_out[0].rearrange("(k p) n -> p k n", p=P)
    w_out_v = w_out[0].rearrange("(k p) n -> p k n", p=P)
    w_r_v = w_r[0].rearrange("h i j -> i h j")
    w_i_v = w_i[0].rearrange("h i j -> i h j")
    x_t_v = x_t.rearrange("(k p) s -> p k s", p=P)
    x_v = x[0].rearrange("(b p) d -> p b d", p=P)
    out_v = out[0].rearrange("(b p) d -> p b d", p=P)
    ds = bass.ds

    with ExitStack() as ctx:
        def sb(name, shape, dt=F32, where=ctx):
            return where.enter_context(nc.sbuf_tensor(name, shape, dt))

        def sem(name):
            return ctx.enter_context(nc.semaphore(name))

        def ps(name, shape):
            return ctx.enter_context(nc.psum_tensor(name, shape, F32))

        bias_rows_d = nc.dram_tensor("bias_rows", [HEADS, P, SPAN], F32, kind="Internal").ap()

        xt_hi = sb("xt_hi", [P, KT, S], F32R)
        xt_lo = sb("xt_lo", [P, KT, S], F32R)
        merged = sb("merged", [P, KT, S])
        raw = sb("raw", [P, 2, 8, P])
        w_hi = sb("w_hi", [P, 4, 4, P], F32R)
        w_lo = sb("w_lo", [P, 4, 4, P], F32R)
        gate_raw = ExitStack()
        gate_w = sb("gate_w", [P, 2, P], where=gate_raw)
        gate_raw.close()
        stats = sb("stats", [P, NB, 4, 6])
        moments = sb("moments", [P, NB, 2])
        spread = sb("spread", [P, NB, 2])
        sb("pad_gate_raw", [P, 2 * P - 28 * NB])
        gate_w_hi = sb("gate_w_hi", [P, 2, P], F32R)
        gate_w_lo = sb("gate_w_lo", [P, 2, P], F32R)
        chan_sb = sb("chan_sb", [P, KT, 8])
        exp_scale = sb("exp_scale", [P, KT])
        tanh_scale = sb("tanh_scale", [P, KT])

        early = ExitStack()
        q_sb = sb("q_sb", [P, NB, AT * P], where=early)
        bias = sb("bias", [P, HEADS, 2 * P], where=early)
        g_attn = sb("g_attn", [P, NB, AT * P], where=early)
        k_sb = sb("k_sb", [P, KV_HEADS, S], where=early)
        v_sb = sb("v_sb", [P, NB, KV_HEADS * HD], where=early)
        sinks_sb = sb("sinks_sb", [P, HEADS], where=early)
        table_sb = sb("table_sb", [BUCKETS, HEADS], where=early)
        bias_table = sb("bias_table", [BUCKETS + 1, HEADS], where=early)
        buckets = sb("buckets", [BUCKETS + 1, SPAN], where=early)
        bias_rows = sb("bias_rows_sb", [HEADS, SPAN], where=early)
        sp = sb("sp", [P, 6, KT], where=early)
        sb("pad", [P, 1024 - 3 * HEADS - 2 * SPAN - 6 * KT], where=early)
        probs = sb("probs", [P, GROUP, 2 * P], where=early)
        probs_t = sb("probs_t", [P, 2, GROUP * P], where=early)
        q_item = sb("q_item", [P, 2 * P], where=early)
        k_item = sb("k_item", [P, 2 * P], where=early)
        v_item = sb("v_item", [P, 2, HD], where=early)
        sig_qg = sb("sig_qg", [P, S], where=early)
        v_t = sb("v_t", [P, KVT, S], where=early)
        ident = sb("ident", [P, P], where=early)
        neg_sinks = sb("neg_sinks", [P, HEADS], where=early)
        small = sb("small", [P, 6, 4], where=early)
        early.close()

        hg_hi = sb("hg_hi", [P, KT, S], F32R)
        hg_lo = sb("hg_lo", [P, KT, S], F32R)
        middle = ExitStack()
        xc = sb("xc", [P, S], where=middle)
        rec_gate = sb("rec_gate", [P, S], where=middle)
        inp = sb("inp", [P, S], where=middle)
        decay = sb("decay", [P, S], where=middle)
        norm = sb("norm", [P, S], where=middle)
        hid = sb("hid", [P, S], where=middle)
        silu = sb("silu", [P, S], where=middle)
        gated = sb("gated", [P, S], where=middle)
        xc_hi = sb("xc_hi", [P, S], F32R, where=middle)
        xc_lo = sb("xc_lo", [P, S], F32R, where=middle)
        middle.close()
        late = ExitStack()
        EARLY = 8
        wo_early = sb("wo_early", [P, EARLY, S], where=late)
        late.close()
        ln_gb = sb("ln_gb", [P, 2, D])
        sig_mr = sb("sig_mr", [P, S])
        mixed_r = sb("mixed_r", [P, S])
        ag_hi, ag_lo = hg_hi[:, 0:AT, :], hg_hi[:, AT:2 * AT, :]

        def raw_quarter(turn, s):
            if isinstance(turn, int) and turn < KVT:
                return raw[:, s // 2, :, :].rearrange("p (k u) n -> p k u n", u=2)[:, :, s % 2, :]
            return raw[:, s // 2, 4 * (s % 2):4 * (s % 2) + 4, :]

        def chunk_source(g, k):
            if isinstance(g, int) and g == 0 and k < EARLY:
                return wo_early[:, k, :]
            return raw[:, k // 2 % 2, 4 * (k % 2):4 * (k % 2) + 4, :].rearrange("p k n -> p (k n)")

        bank_a = ps("bank_a", [P, S])
        bank_b = ps("bank_b", [P, S])
        bank_s = ps("bank_s", [P, 2, S])
        bank_t = ps("bank_t", [P, 2, S])
        bank_o = ps("bank_o", [P, S])
        scores = bank_s[:, :, :].rearrange("p a (h k) -> p (a h) k", h=2)
        out_banks = [bank_s[:, 0, :], bank_s[:, 1, :], bank_t[:, 0, :], bank_t[:, 1, :]]

        raw_landed = [sem("raw_landed0"), sem("raw_landed1")]
        hi_ready = sem("hi_ready")
        lo_ready = sem("lo_ready")
        multiplied = sem("multiplied")
        a_free = sem("a_free")
        b_free = sem("b_free")
        X_CUTS = [0, 1, 2, 4, 8, 12, 16]
        x_landed = [sem(f"x_landed{i}") for i in range(len(X_CUTS) - 1)]
        xt_hi_ready = sem("xt_hi_ready")
        xt_lo_ready = sem("xt_lo_ready")
        chan_landed = sem("chan_landed")
        sinks_landed = sem("sinks_landed")
        table_landed = sem("table_landed")
        table_filled = sem("table_filled")
        sinks_ready = sem("sinks_ready")
        soft_step = sem("soft_step")
        soft_exp = sem("soft_exp")
        scales_ready = sem("scales_ready")
        rows_done = sem("rows_done")
        rows_copied = sem("rows_copied")
        rows_stored = sem("rows_stored")
        bias_landed = sem("bias_landed")
        ident_zero = sem("ident_zero")
        ident_ready = sem("ident_ready")
        k_saved = sem("k_saved")
        vt_saved = sem("vt_saved")
        v_turned = sem("v_turned")
        v_saved = sem("v_saved")
        sig_qg_ready = sem("sig_qg_ready")
        qk_staged = sem("qk_staged")
        v_staged = sem("v_staged")
        scores_done = sem("scores_done")
        prev_masked = sem("prev_masked")
        biased = sem("biased")
        row_max = sem("row_max")
        shift_ready = sem("shift_ready")
        sink_shifted = sem("sink_shifted")
        exp_done = sem("exp_done")
        denom_ready = sem("denom_ready")
        recip_ready = sem("recip_ready")
        probs_ready = sem("probs_ready")
        turned = sem("turned")
        turned_saved = sem("turned_saved")
        pv_done = sem("pv_done")
        attn_gated = sem("attn_gated")
        ag_hi_ready = sem("ag_hi_ready")
        ag_lo_ready = sem("ag_lo_ready")
        attn_mixed = sem("attn_mixed")
        gate_w_landed = sem("gate_w_landed")
        conv_begun = sem("conv_begun")
        conv_tap = sem("conv_tap")
        gate_w_hi_ready = sem("gate_w_hi_ready")
        gate_w_lo_ready = sem("gate_w_lo_ready")
        xc_hi_ready = sem("xc_hi_ready")
        xc_lo_ready = sem("xc_lo_ready")
        gates_done = sem("gates_done")
        sig_r_ready = sem("sig_r_ready")
        sig_i_ready = sem("sig_i_ready")
        gated_x = sem("gated_x")
        decay_ready = sem("decay_ready")
        tanh_ready = sem("tanh_ready")
        decay_sq = sem("decay_sq")
        norm_sq = sem("norm_sq")
        norm_ready = sem("norm_ready")
        drive_ready = sem("drive_ready")
        scan_done = sem("scan_done")
        sig_gr_ready = sem("sig_gr_ready")
        branch_ready = sem("branch_ready")
        hg_hi_ready = sem("hg_hi_ready")
        hg_lo_ready = sem("hg_lo_ready")
        sig_mr_ready = sem("sig_mr_ready")
        mixed_r_ready = sem("mixed_r_ready")
        merged_ready = sem("merged_ready")
        mg_hi_ready = sem("mg_hi_ready")
        mg_lo_ready = sem("mg_lo_ready")
        chunk_hi_ready = sem("chunk_hi_ready")
        chunk_lo_ready = sem("chunk_lo_ready")
        early_landed = sem("early_landed")
        ln_landed = sem("ln_landed")
        res_landed = [sem(f"res_landed{s}") for s in range(NB)]
        wo_released = sem("wo_released")
        rows_summed = sem("rows_summed")
        z_ready = sem("z_ready")
        stats_ready = sem("stats_ready")
        mom_ready = sem("mom_ready")
        var_ready = sem("var_ready")
        std_ready = sem("std_ready")
        rstd_ready = sem("rstd_ready")
        centred = sem("centred")
        normed = sem("normed")
        stored = sem("stored")

        block = ctx.enter_context(nc.Block())

        @block.sync
        def _(sp_eng):
            def load_half(turn, half, src):
                if not (isinstance(turn, int) and turn == 0):
                    sp_eng.wait_ge(lo_ready, 4 * turn + 2 * half - 2)
                shape = raw[:, half, :, :]
                if src.shape[1] != 8:
                    shape = shape.rearrange("p (k a) n -> p k (a n)", k=src.shape[1])
                sp_eng.dma_start(shape, src).then_inc(raw_landed[half], 16)

            def load_turn(turn, src_v, col):
                for half in range(2):
                    load_half(turn, half, src_v[:, 8 * half:8 * half + 8, ds(col, P)])

            for u in range(KVT):
                for half in range(2):
                    k = 4 * (2 * u + half)
                    load_half(T_VK + u, half, w_in_v[:, k:k + 4, COL_V:COL_V + KVT * P])
            for u in range(KVT):
                load_turn(T_VK + KVT + u, w_in_v, COL_K + P * u)
            with sp_eng.Fori(0, AT) as j:
                load_turn(T_QG + 2 * j, w_in_v, COL_Q + P * j)
                load_turn(T_QG + 1 + 2 * j, w_in_v, COL_GA + P * j)
            with sp_eng.Fori(0, KT) as c:
                load_turn(T_MA + c, w_in_v, COL_MA + P * c)
            load_turn(T_X0, w_in_v, COL_X)
            with sp_eng.Fori(0, KT // 2) as c:
                for half in range(2):
                    load_half(T_AO + c, half, w_ao_v[:, :, ds(2 * P * c + P * half, P)])

            def load_gate_weights(c):
                sp_eng.wait_ge(multiplied, 4 * T_RN - 3 + 8 * c)
                sp_eng.dma_start(gate_w[:, 0:1, :], w_r_v[:, ds(c, 1), :]).then_inc(gate_w_landed, 16)
                sp_eng.dma_start(gate_w[:, 1:2, :], w_i_v[:, ds(c, 1), :]).then_inc(gate_w_landed, 16)

            with sp_eng.Fori(0, KT - 1) as c:
                load_turn(T_RN + 2 * c, w_in_v, COL_GR + P * c)
                load_gate_weights(c)
                load_turn(T_RN + 1 + 2 * c, w_in_v, COL_X + P + P * c)
            load_turn(T_RN + 2 * KT - 2, w_in_v, COL_GR + P * (KT - 1))
            load_gate_weights(KT - 1)
            with sp_eng.Fori(1, KT + 1) as n:
                load_turn(T_MX - 2 + 2 * n, w_in_v, COL_MR - P + P * n)
                load_turn(T_MX - 1 + 2 * n, w_ro_v, P * n - P)
            def load_chunks(h, columns, ready, count):
                sp_eng.wait_ge(ready, count)
                sp_eng.dma_start(raw[:, h % 2, :, :].rearrange("p (k a) n -> p k (a n)", k=2),
                                 w_out_v[:, 2 * h:2 * h + 2, columns]).then_inc(raw_landed[h % 2], 16)

            for h in range(EARLY // 2, EARLY // 2 + 2):
                load_chunks(h, slice(0, S), lo_ready, 4 * T_WO - 2 + 2 * (h % 2))
            for h in range(EARLY // 2 + 2, KT // 2):
                load_chunks(h, slice(0, S), chunk_lo_ready, 2 * h - 2)
            with sp_eng.Fori(1, 4) as g:
                for h in range(KT // 2):
                    load_chunks(h, ds(S * g, S), chunk_lo_ready, KT * g + 2 * h - 2)
            for s in range(NB):
                parts = 4 if s == NB - 1 else 1
                for i in range(parts):
                    n = D // parts
                    sp_eng.wait_ge(normed, 4 * s + 4 * (i + 1) // parts)
                    sp_eng.dma_start(out_v[:, s, i * n:(i + 1) * n],
                                     merged[:, 4 * s:4 * s + 4, :].rearrange("p a n -> p (a n)")[:, i * n:(i + 1) * n]
                                     ).then_inc(stored, 16)
            sp_eng.wait_ge(stored, 16 * (NB + 3))

        @block.gpsimd
        def _(pool):
            nc.gpsimd.memset(ident[:, :], 0.0).then_inc(ident_zero, 1)
            pool.wait_ge(ident_zero, 1)
            nc.gpsimd.affine_select(out=ident[:, :], in_=ident[:, :], compare_op=ALU.not_equal, fill=1.0,
                                    base=0, pattern=[[-1, P]], channel_multiplier=1).then_inc(ident_ready, 1)
            pool.wait_ge(rows_copied, 1)
            pool.dma_start(bias_rows_d, bias_rows[:, :].unsqueeze(1).broadcast_to([HEADS, P, SPAN])
                           ).then_inc(rows_stored, 16)
            pool.wait_ge(rows_stored, 16)
            pool.dma_start(bias[:, :, :], bass.AP(tensor=bias_rows_d.tensor, offset=P - 1,
                                                  ap=[[SPAN - 1, P], [P * SPAN, HEADS], [1, 2 * P]])).then_inc(bias_landed, 16)

            def stage(i, b, g, first_block, first):
                if first:
                    pool.wait_ge(a_free, A_MA)
                    pool.wait_ge(k_saved, 4 * KVT)
                else:
                    pool.wait_ge(scores_done, 2 * i)
                nc.gpsimd.tensor_copy(q_item[:, :], q_sb[:, :, :].rearrange("p b n -> p (b n)")[:, ds(2 * P * i, 2 * P)]
                                      ).then_inc(qk_staged, 1)
                keys = k_sb[:, :, :].rearrange("p g s -> p (g s)")
                if first_block:
                    nc.gpsimd.tensor_copy(k_item[:, 0:P], keys[:, ds(S * g, P)]).then_inc(qk_staged, 1)
                    nc.gpsimd.tensor_copy(k_item[:, P:2 * P], keys[:, ds(S * g, P)]).then_inc(qk_staged, 1)
                else:
                    nc.gpsimd.tensor_copy(k_item[:, :], keys[:, ds(S * g + P * b - P, 2 * P)]).then_inc(qk_staged, 2)
                if first:
                    pool.wait_ge(v_saved, KVT)
                else:
                    pool.wait_ge(pv_done, i)
                values = v_sb[:, :, :].rearrange("p b n -> p (b n)")
                row = KV_HEADS * HD
                last = 0 if first_block else 1
                nc.gpsimd.tensor_copy(v_item[:, 0, :], values[:, ds(row * b + HD * g - row * last, HD)]).then_inc(v_staged, 1)
                nc.gpsimd.tensor_copy(v_item[:, 1, :], values[:, ds(row * b + HD * g, HD)]).then_inc(v_staged, 1)

            stage(0, 0, 0, True, True)
            with pool.Fori(1, KV_HEADS) as g:
                stage(g, 0, g, True, False)
            with pool.Fori(1, NB) as b:
                with pool.Fori(0, KV_HEADS) as g:
                    stage(4 * b + g, b, g, False, False)

            pool.wait_ge(hg_lo_ready, KT)
            for k in range(0, EARLY, 4):
                pool.dma_start(wo_early[:, k:k + 4, :], w_out_v[:, k:k + 4, 0:S]).then_inc(early_landed, 16)
            pool.wait_ge(chunk_lo_ready, EARLY)
            pool.dma_start(ln_gb[:, 0, :], ln_g.partition_broadcast(P)).then_inc(ln_landed, 16)
            pool.dma_start(ln_gb[:, 1, :], ln_b.partition_broadcast(P)).then_inc(ln_landed, 16)
            pool.wait_ge(mg_lo_ready, KT)
            for s in range(NB):
                pool.dma_start(merged[:, 4 * s:4 * s + 4, :].rearrange("p a n -> p (a n)"), x_v[:, s, :]
                               ).then_inc(res_landed[s], 16)

        @block.scalar
        def _(act):
            for i in range(len(x_landed)):
                a, b = X_CUTS[i], X_CUTS[i + 1]
                act.dma_start(merged[:, a:b, :], x_t_v[:, a:b, :]).then_inc(x_landed[i], 16)
            act.dma_start(chan_sb[:, :, :], chan).then_inc(chan_landed, 16)
            act.dma_start(sinks_sb[:, :], sinks[0].partition_broadcast(P)).then_inc(sinks_landed, 16)
            act.dma_start(table_sb[:, :], rel_bias).then_inc(table_landed, 16)
            act.dma_start(buckets[:, :], bucket_rows).then_inc(table_landed, 16)

            def high_parts(turn, quarters):
                for s in quarters:
                    if s % 2 == 0:
                        act.wait_ge(raw_landed[s // 2], 16 * turn + 16)
                    if not (isinstance(turn, int) and turn == 0):
                        act.wait_ge(multiplied, 4 * turn + s - 3)
                    nc.scalar.activation(w_hi[:, s, :, :], raw_quarter(turn, s), ACT.Copy
                                         ).then_inc(hi_ready, 1)

            def high_chunk(g, k):
                if isinstance(g, int) and g == 0:
                    if k < EARLY:
                        act.wait_ge(early_landed, 32)
                    elif k % 2 == 0:
                        act.wait_ge(raw_landed[k // 2 % 2], 16 * (T_WO + 1 + (k - EARLY) // 4))
                    act.wait_ge(multiplied, 4 * (T_WO - 2) + k // 4 + 1)
                else:
                    if k % 2 == 0:
                        act.wait_ge(raw_landed[k // 2 % 2], 16 * (T_WO - 2 + k // 4 + 1) + 64 * g)
                    act.wait_ge(wo_released, KT * g - KT + k + 1)
                nc.scalar.activation(xt_hi[:, k, :], chunk_source(g, k), ACT.Copy).then_inc(chunk_hi_ready, 1)

            for k in range(KT):
                if k % 4 == 0:
                    high_parts(k // 8, [k // 2 % 4])
                if k in X_CUTS:
                    act.wait_ge(x_landed[X_CUTS.index(k)], 16)
                nc.scalar.activation(xt_hi[:, k, :], merged[:, k, :], ACT.Copy).then_inc(xt_hi_ready, 1)
                if k % 4 == 3:
                    high_parts(k // 8, [k // 2 % 4])
            for u in range(KVT, 2 * KVT + 1):
                high_parts(T_VK + u, range(4))
            act.wait_ge(soft_step, 2)
            nc.scalar.activation(sp[:, 1, :], sp[:, 1, :], ACT.Exp).then_inc(soft_exp, 1)

            with act.Fori(0, AT) as j:
                high_parts(T_QG + 1 + 2 * j, range(4))
                high_parts(T_QG + 2 + 2 * j, range(4))
                act.wait_ge(multiplied, 4 * T_QG + 8 + 8 * j)
                nc.scalar.activation(sig_qg[:, :], bank_b[:, :], ACT.Sigmoid).then_inc(sig_qg_ready, 1)

            def attention_item(i):
                act.wait_ge(sink_shifted, i + 1)
                nc.scalar.activation(small[:, 3, :], small[:, 2, :], ACT.Exp).then_inc(exp_done, 1)
                for h in range(GROUP):
                    nc.scalar.activation(probs[:, h, :], probs[:, h, :], ACT.Exp, bias=small[:, 1, h:h + 1],
                                         accum_out=small[:, 4, h:h + 1]).then_inc(exp_done, 1)
                high_parts(T_MA + 1 + i, range(4))
                act.wait_ge(multiplied, 4 * T_MA + 4 + 4 * i)
                nc.scalar.activation(merged[:, ds(i, 1), :], bank_a[:, :].unsqueeze(1), ACT.Sigmoid).then_inc(a_free, 1)

            with act.Fori(0, ITEMS) as i:
                attention_item(i)

            def gated_high(k):
                nc.scalar.activation(ag_hi[:, k, :].rearrange("p (b n) -> p b n", b=NB),
                                     g_attn[:, :, k * P:(k + 1) * P], ACT.Copy).then_inc(ag_hi_ready, 1)

            act.wait_ge(attn_gated, ITEMS - 1)
            for k in range(AT - 2):
                gated_high(k)
            high_parts(T_AO, [0])
            act.wait_ge(attn_gated, ITEMS)
            for k in range(AT - 2, AT):
                gated_high(k)
            high_parts(T_AO, [1, 2, 3])

            def convolution_begin(c):
                if isinstance(c, int) and c == 0:
                    act.wait_ge(multiplied, 4 * T_X0 + 4)
                    bank = bank_s[:, 0, :]
                else:
                    act.wait_ge(multiplied, 4 * T_RN + 8 * c)
                    act.wait_ge(gated_x, c)
                    bank = bank_a[:, :]
                nc.scalar.activation(xc[:, :], bank, ACT.Identity, scale=chan_sb[:, ds(c, 1), 3],
                                     bias=chan_sb[:, ds(c, 1), 4]).then_inc(conv_begun, 1)

            def gate_operands_high(c):
                act.wait_ge(gate_w_landed, 32 * c + 32)
                nc.scalar.activation(gate_w_hi[:, :, :], gate_w[:, :, :], ACT.Copy).then_inc(gate_w_hi_ready, 1)
                act.wait_ge(conv_tap, 3 * c + 3)
                nc.scalar.activation(xc_hi[:, :], xc[:, :], ACT.Copy).then_inc(xc_hi_ready, 1)

            def gate_sigmoids(c):
                act.wait_ge(gates_done, c + 1)
                nc.scalar.activation(rec_gate[:, :], bank_s[:, 0, :], ACT.Sigmoid, bias=chan_sb[:, ds(c, 1), 5]
                                     ).then_inc(sig_r_ready, 1)
                nc.scalar.activation(inp[:, :], bank_s[:, 1, :], ACT.Sigmoid, bias=chan_sb[:, ds(c, 1), 6]
                                     ).then_inc(sig_i_ready, 1)

            def decays(c):
                act.wait_ge(sig_r_ready, c + 1)
                nc.scalar.activation(decay[:, :], rec_gate[:, :], ACT.Exp, scale=exp_scale[:, ds(c, 1)]
                                     ).then_inc(decay_ready, 1)
                nc.scalar.activation(norm[:, :], rec_gate[:, :], ACT.Tanh, scale=tanh_scale[:, ds(c, 1)]
                                     ).then_inc(tanh_ready, 1)

            def norm_root(c):
                act.wait_ge(norm_sq, c + 1)
                nc.scalar.activation(norm[:, :], norm[:, :], ACT.Sqrt).then_inc(norm_ready, 1)

            def branch_high(c):
                act.wait_ge(branch_ready, c + 1)
                nc.scalar.activation(hg_hi[:, ds(c, 1), :], gated[:, :].unsqueeze(1), ACT.Copy).then_inc(hg_hi_ready, 1)

            def recurrent_gates(c, first=False):
                gate_operands_high(c)
                high_parts(T_RN + 1 + 2 * c, [0, 1])
                if not first:
                    branch_high(c - 1)
                high_parts(T_RN + 1 + 2 * c, [2])
                gate_sigmoids(c)
                high_parts(T_RN + 1 + 2 * c, [3])
                act.wait_ge(multiplied, 4 * T_RN + 4 + 8 * c)
                nc.scalar.activation(silu[:, :], bank_b[:, :], ACT.Sigmoid).then_inc(sig_gr_ready, 1)

            def recurrent_decay(c):
                high_parts(T_RN + 2 + 2 * c, [0])
                decays(c)
                high_parts(T_RN + 2 + 2 * c, [1, 2])
                norm_root(c)
                high_parts(T_RN + 2 + 2 * c, [3])

            convolution_begin(0)
            with act.Fori(0, KT // 2) as c:
                high_parts(T_AO + 1 + c, range(4))
            recurrent_gates(0, first=True)
            recurrent_decay(0)
            convolution_begin(1)
            with act.Fori(1, KT - 1) as c:
                recurrent_gates(c)
                recurrent_decay(c)
                convolution_begin(c + 1)
            recurrent_gates(KT - 1)

            def merge_tile(c, first=False, last=False):
                if first:
                    recurrent_decay(KT - 1)
                    branch_high(KT - 1)
                else:
                    for s in range(4):
                        high_parts(T_MX + 1 + 2 * c, [s])
                        if last:
                            high_chunk(0, 2 * s)
                            high_chunk(0, 2 * s + 1)
                    act.wait_ge(mixed_r_ready, c)
                act.wait_ge(multiplied, 4 * T_MX + 4 + 8 * c)
                nc.scalar.activation(sig_mr[:, :], bank_a[:, :], ACT.Sigmoid).then_inc(sig_mr_ready, 1)
                if not last:
                    high_parts(T_MX + 2 + 2 * c, range(4))

            merge_tile(0, first=True)
            with act.Fori(1, KT - 1) as c:
                merge_tile(c)
            merge_tile(KT - 1, last=True)

            def merged_high(k):
                act.wait_ge(multiplied, 4 * (T_WO - 1) + k // 4 + 1)
                act.wait_ge(merged_ready, k + 1)
                nc.scalar.activation(hg_hi[:, k, :], merged[:, k, :], ACT.Copy).then_inc(mg_hi_ready, 1)

            for k in range(8):
                high_chunk(0, 8 + k)
                merged_high(k)
            for k in range(8, KT):
                merged_high(k)
            with act.Fori(1, 4) as g:
                for k in range(KT):
                    high_chunk(g, k)
            for s in range(NB):
                act.wait_ge(var_ready, s + 1)
                nc.scalar.activation(spread[:, s, 0:1], moments[:, s, 1:2], ACT.Sqrt).then_inc(std_ready, 1)

        @block.vector
        def _(dve):
            V = nc.vector

            def low_parts(turn, quarters):
                for s in quarters:
                    dve.wait_ge(hi_ready, 4 * turn + s + 1)
                    V.tensor_tensor(w_lo[:, s, :, :], raw_quarter(turn, s), w_hi[:, s, :, :], ALU.subtract
                                    ).then_inc(lo_ready, 1)

            def low_chunk(g, k):
                dve.wait_ge(chunk_hi_ready, KT * g + k + 1)
                V.tensor_tensor(xt_lo[:, k, :], chunk_source(g, k), xt_hi[:, k, :], ALU.subtract
                                ).then_inc(chunk_lo_ready, 1)

            V.memset(bias_table[BUCKETS:BUCKETS + 1, :], NEG_INF).then_inc(table_filled, 1)
            for k in range(KT):
                if k % 4 == 0:
                    low_parts(k // 8, [k // 2 % 4])
                dve.wait_ge(xt_hi_ready, k + 1)
                V.tensor_tensor(xt_lo[:, k, :], merged[:, k, :], xt_hi[:, k, :], ALU.subtract).then_inc(xt_lo_ready, 1)
                if k % 4 == 3:
                    low_parts(k // 8, [k // 2 % 4])
            dve.wait_ge(table_landed, 32)
            V.tensor_copy(bias_table[0:BUCKETS, :].rearrange("p (g h t) -> p g h t", t=2, h=2),
                          table_sb[:, :].rearrange("p (g t h) -> p g h t", t=2, h=2)).then_inc(table_filled, 1)


            low_parts(T_VK + KVT, range(4))
            for u, bank, free in ((0, bank_a, a_free), (1, bank_b, b_free)):
                dve.wait_ge(multiplied, 7 + u)
                V.tensor_copy(v_t[:, u, :], bank[:, :]).then_inc(free, 1)
            dve.wait_ge(rows_done, 1)
            V.tensor_copy(bias_rows[:, :], bank_o[0:HEADS, 0:SPAN]).then_inc(rows_copied, 1)

            def save_keys(u, bank, free):
                dve.wait_ge(multiplied, 4 * (T_VK + KVT + u) + 4)
                for head in range(2):
                    for half in range(2):
                        V.tensor_copy(k_sb[64 * half:64 * half + 64, 2 * u + head, :],
                                      bank[64 * head:64 * head + 64, :]).then_inc(k_saved, 1)
                dve.wait_ge(k_saved, 4 * (u + 1))
                dve.sem_inc(free, 1)

            low_parts(T_VK + KVT + 1, range(4))
            save_keys(0, bank_a, a_free)
            for t in range(KVT):
                dve.wait_ge(v_turned, t + 1)
                V.tensor_copy(v_sb[:, :, t * P:(t + 1) * P], bank_t[:, t, :].rearrange("p (b n) -> p b n", b=NB)
                              ).then_inc(v_saved, 1)
            low_parts(T_QG, range(4))
            save_keys(1, bank_b, b_free)

            steps = 0

            def then_next(ins):
                nonlocal steps
                steps += 1
                ins.then_inc(soft_step, 1)
                dve.wait_ge(soft_step, steps)

            lam, negated, e, z, z2, acc = chan_sb[:, :, 7], sp[:, 0, :], sp[:, 1, :], sp[:, 2, :], sp[:, 3, :], sp[:, 4, :]
            dve.wait_ge(chan_landed, 16)
            then_next(V.tensor_scalar(negated, lam, -1.0, None, ALU.mult))
            then_next(V.tensor_tensor(e, negated, lam, ALU.min))
            dve.wait_ge(soft_exp, 1)
            then_next(V.tensor_scalar(z, e, 2.0, None, ALU.add))
            then_next(V.reciprocal(acc, z))
            then_next(V.tensor_tensor(z, e, acc, ALU.mult))
            then_next(V.tensor_tensor(z2, z, z, ALU.mult))
            then_next(V.tensor_scalar(acc, z2, 1.0 / 17, None, ALU.mult))
            for n in (15, 13, 11, 9, 7, 5, 3):
                then_next(V.scalar_tensor_tensor(acc, acc, 1.0 / n, z2, ALU.add, ALU.mult))
            then_next(V.scalar_tensor_tensor(acc, acc, 1.0, z, ALU.add, ALU.mult))
            then_next(V.tensor_scalar(negated, negated, 0.0, None, ALU.max))
            then_next(V.scalar_tensor_tensor(acc, acc, 2.0, negated, ALU.mult, ALU.add))
            V.tensor_scalar(exp_scale[:, :], acc, -LRU_C, None, ALU.mult).then_inc(scales_ready, 1)
            V.tensor_scalar(tanh_scale[:, :], acc, LRU_C, None, ALU.mult).then_inc(scales_ready, 1)
            dve.wait_ge(sinks_landed, 16)
            V.tensor_scalar(neg_sinks[:, :].rearrange("p (g h t) -> p g h t", t=2, h=2),
                            sinks_sb[:, :].rearrange("p (g t h) -> p g h t", t=2, h=2), -1.0, None, ALU.mult).then_inc(sinks_ready, 1)


            with dve.Fori(0, AT) as j:
                low_parts(T_QG + 1 + 2 * j, range(4))
                dve.wait_ge(multiplied, 4 * T_QG + 4 + 8 * j)
                V.tensor_copy(q_sb[:, :, ds(P * j, P)], bank_a[:, :].rearrange("p (b n) -> p b n", b=NB)
                              ).then_inc(a_free, 1)
                low_parts(T_QG + 2 + 2 * j, range(4))
                dve.wait_ge(sig_qg_ready, j + 1)
                V.tensor_tensor(g_attn[:, :, ds(P * j, P)], bank_b[:, :].rearrange("p (b n) -> p b n", b=NB),
                                sig_qg[:, :].rearrange("p (b n) -> p b n", b=NB), ALU.mult).then_inc(b_free, 1)

            def gate_item(i):
                dve.wait_ge(pv_done, i + 1)
                place = g_attn[:, :, :].rearrange("p b n -> p (b n)")[:, ds(2 * P * i, 2 * P)]
                V.tensor_tensor(place, bank_o[:, 0:2 * P], place, ALU.mult).then_inc(attn_gated, 1)

            def attention_item(i, g, first_block, first):
                dve.wait_ge(scores_done, 2 * i + 2)
                if first_block:
                    V.memset(probs[:, :, 0:P], NEG_INF).then_inc(prev_masked, 1)
                    V.scalar_tensor_tensor(probs[:, :, P:2 * P], scores[:, :, P:2 * P], SCALE,
                                           bias[:, ds(GROUP * g, GROUP), P:2 * P], ALU.mult, ALU.add).then_inc(biased, 1)
                    dve.wait_ge(prev_masked, i + 1)
                else:
                    V.scalar_tensor_tensor(probs[:, :, :], scores, SCALE, bias[:, ds(GROUP * g, GROUP), :],
                                           ALU.mult, ALU.add).then_inc(biased, 1)
                dve.wait_ge(biased, i + 1)
                V.tensor_reduce(small[:, 0, :], probs[:, :, :], AX.X, ALU.max).then_inc(row_max, 1)
                dve.wait_ge(row_max, i + 1)
                V.scalar_tensor_tensor(small[:, 1, :], small[:, 0, :], -1.0, neg_sinks[:, ds(GROUP * g, GROUP)],
                                       ALU.mult, ALU.min).then_inc(shift_ready, 1)
                dve.wait_ge(shift_ready, i + 1)
                V.tensor_tensor(small[:, 2, :], small[:, 1, :], neg_sinks[:, ds(GROUP * g, GROUP)], ALU.subtract
                                ).then_inc(sink_shifted, 1)
                low_parts(T_MA + 1 + i, [0])
                if not first:
                    gate_item(i - 1)
                low_parts(T_MA + 1 + i, [1])
                dve.wait_ge(exp_done, 5 * i + 5)
                V.tensor_tensor(small[:, 4, :], small[:, 4, :], small[:, 3, :], ALU.add).then_inc(denom_ready, 1)
                dve.wait_ge(denom_ready, i + 1)
                V.reciprocal(small[:, 5, :], small[:, 4, :]).then_inc(recip_ready, 1)
                dve.wait_ge(recip_ready, i + 1)
                V.tensor_tensor(probs[:, :, :], probs[:, :, :],
                                small[:, 5, :].unsqueeze(2).broadcast_to([P, GROUP, 2 * P]), ALU.mult
                                ).then_inc(probs_ready, 1)
                low_parts(T_MA + 1 + i, [2, 3])
                for w in range(2):
                    dve.wait_ge(turned, 2 * i + w + 1)
                    V.tensor_copy(probs_t[:, w, :], bank_t[:, w, :]).then_inc(turned_saved, 1)

            dve.wait_ge(bias_landed, 16)
            dve.wait_ge(sinks_ready, 1)
            attention_item(0, 0, True, True)
            with dve.Fori(1, KV_HEADS) as g:
                attention_item(g, g, True, False)
            with dve.Fori(1, NB) as b:
                with dve.Fori(0, KV_HEADS) as g:
                    attention_item(4 * b + g, g, False, False)

            def gated_low(k):
                dve.wait_ge(ag_hi_ready, k + 1)
                V.tensor_tensor(ag_lo[:, k, :].rearrange("p (b n) -> p b n", b=NB), g_attn[:, :, k * P:(k + 1) * P],
                                ag_hi[:, k, :].rearrange("p (b n) -> p b n", b=NB), ALU.subtract).then_inc(ag_lo_ready, 1)

            def convolution_taps(c):
                dve.wait_ge(conv_begun, c + 1)
                first = isinstance(c, int) and c == 0
                bank = bank_s[:, 0, :] if first else bank_a[:, :]
                for tap in range(3):
                    back = tap + 1
                    if tap:
                        dve.wait_ge(conv_tap, 3 * c + tap)
                    V.scalar_tensor_tensor(xc[:, back:S], bank[:, 0:S - back], chan_sb[:, ds(c, 1), 3 - back],
                                           xc[:, back:S], ALU.mult, ALU.add).then_inc(conv_tap, 1)
                if not first:
                    dve.wait_ge(conv_tap, 3 * c + 3)
                    dve.sem_inc(a_free, 1)

            for k in range(AT - 2):
                gated_low(k)
            low_parts(T_AO, [0])
            gate_item(ITEMS - 1)
            for k in range(AT - 2, AT):
                gated_low(k)
            low_parts(T_AO, [1, 2, 3])
            convolution_taps(0)
            dve.wait_ge(a_free, A_AO)
            with dve.Fori(0, KT // 2) as c:
                for bank, free, half in ((bank_b, b_free, 0), (bank_a, a_free, 1)):
                    low_parts(T_AO + 1 + c, [2 * half, 2 * half + 1])
                    dve.wait_ge(multiplied, 4 * T_AO + 2 + 2 * half + 4 * c)
                    V.tensor_tensor(merged[:, ds(2 * c + half, 1), :], bank[:, :].unsqueeze(1),
                                    merged[:, ds(2 * c + half, 1), :], ALU.mult).then_inc(free, 1)

            def drive_input(c):
                dve.wait_ge(sig_i_ready, c + 1)
                V.tensor_tensor(inp[:, :], inp[:, :], xc[:, :], ALU.mult).then_inc(gated_x, 1)

            def norm_square(c):
                dve.wait_ge(decay_ready, c + 1)
                V.tensor_tensor(hid[:, :], decay[:, :], decay[:, :], ALU.mult).then_inc(decay_sq, 1)
                dve.wait_ge(decay_sq, c + 1)
                dve.wait_ge(tanh_ready, c + 1)
                V.scalar_tensor_tensor(norm[:, :], hid[:, :], 1.0, norm[:, :], ALU.add, ALU.mult).then_inc(norm_sq, 1)

            def recurrence(c):
                dve.wait_ge(norm_ready, c + 1)
                dve.wait_ge(gated_x, c + 1)
                V.tensor_tensor(inp[:, :], inp[:, :], norm[:, :], ALU.mult).then_inc(drive_ready, 1)
                dve.wait_ge(drive_ready, c + 1)
                V.tensor_tensor_scan(hid[:, :], decay[:, :], inp[:, :], 0.0, ALU.mult, ALU.add).then_inc(scan_done, 1)
                dve.wait_ge(scan_done, c + 1)
                dve.wait_ge(b_free, B_RN + 1 + c)
                V.tensor_tensor(gated[:, :], hid[:, :], silu[:, :], ALU.mult).then_inc(branch_ready, 1)

            def branch_low(c):
                dve.wait_ge(hg_hi_ready, c + 1)
                V.tensor_tensor(hg_lo[:, ds(c, 1), :], gated[:, :].unsqueeze(1), hg_hi[:, ds(c, 1), :], ALU.subtract
                                ).then_inc(hg_lo_ready, 1)

            def recurrent_gates(c, first=False):
                dve.wait_ge(gate_w_hi_ready, c + 1)
                V.tensor_tensor(gate_w_lo[:, :, :], gate_w[:, :, :], gate_w_hi[:, :, :], ALU.subtract
                                ).then_inc(gate_w_lo_ready, 1)
                dve.wait_ge(xc_hi_ready, c + 1)
                V.tensor_tensor(xc_lo[:, :], xc[:, :], xc_hi[:, :], ALU.subtract).then_inc(xc_lo_ready, 1)
                low_parts(T_RN + 1 + 2 * c, [0])
                if not first:
                    recurrence(c - 1)
                low_parts(T_RN + 1 + 2 * c, [1])
                if not first:
                    branch_low(c - 1)
                low_parts(T_RN + 1 + 2 * c, [2, 3])
                dve.wait_ge(sig_gr_ready, c + 1)
                V.tensor_tensor(silu[:, :], bank_b[:, :], silu[:, :], ALU.mult).then_inc(b_free, 1)
                drive_input(c)

            def recurrent_decay(c):
                low_parts(T_RN + 2 + 2 * c, [0, 1])
                norm_square(c)
                low_parts(T_RN + 2 + 2 * c, [2, 3])
                convolution_taps(c + 1)

            recurrent_gates(0, first=True)
            recurrent_decay(0)
            with dve.Fori(1, KT - 1) as c:
                recurrent_gates(c)
                recurrent_decay(c)
            recurrent_gates(KT - 1)

            def add_branches(c):
                dve.wait_ge(sig_mr_ready, c + 1)
                dve.wait_ge(multiplied, 4 * T_MX + 8 + 8 * c)
                V.tensor_tensor(mixed_r[:, :], bank_b[:, :], sig_mr[:, :], ALU.mult).then_inc(mixed_r_ready, 1)
                dve.wait_ge(mixed_r_ready, c + 1)
                V.tensor_tensor(merged[:, ds(c, 1), :], merged[:, ds(c, 1), :], mixed_r[:, :].unsqueeze(1), ALU.add
                                ).then_inc(merged_ready, 1)

            low_parts(T_MX + 1, [0, 1])
            norm_square(KT - 1)
            low_parts(T_MX + 1, [2])
            recurrence(KT - 1)
            low_parts(T_MX + 1, [3])
            branch_low(KT - 1)
            low_parts(T_MX + 2, range(4))
            add_branches(0)
            with dve.Fori(1, KT - 1) as c:
                low_parts(T_MX + 1 + 2 * c, range(4))
                low_parts(T_MX + 2 + 2 * c, range(4))
                add_branches(c)
            for s in range(4):
                low_parts(T_WO - 1, [s])
                low_chunk(0, 2 * s)
                low_chunk(0, 2 * s + 1)

            def merged_low(k):
                dve.wait_ge(mg_hi_ready, k + 1)
                V.tensor_tensor(hg_lo[:, k, :], merged[:, k, :], hg_hi[:, k, :], ALU.subtract).then_inc(mg_lo_ready, 1)

            for k in range(8):
                low_chunk(0, 8 + k)
                merged_low(k)
            add_branches(KT - 1)
            for k in range(8, KT):
                merged_low(k)

            z_rows = [merged[:, 4 * s:4 * s + 4, :] for s in range(NB)]

            def add_residual(g, s):
                if isinstance(g, int) and g == 0:
                    dve.wait_ge(res_landed[s], 16)
                dve.wait_ge(rows_summed, NB * g + s + 1)
                z = merged[:, ds(4 * s + g, 1), :]
                V.scalar_tensor_tensor(z, z, ALPHA, out_banks[s].unsqueeze(1), ALU.mult, ALU.add).then_inc(z_ready, 1)
                dve.wait_ge(z_ready, NB * g + s + 1)
                V.bn_stats(stats[:, s, ds(g, 1), :].rearrange("p a n -> p (a n)"), z.rearrange("p a n -> p (a n)")
                           ).then_inc(stats_ready, 1)

            def normalise(s):
                dve.wait_ge(stats_ready, NB * 3 + s + 1)
                V.bn_aggr(moments[:, s, :], stats[:, s, :, :].rearrange("p a n -> p (a n)")).then_inc(mom_ready, 1)
                dve.wait_ge(mom_ready, s + 1)
                V.tensor_scalar(moments[:, s, 1:2], moments[:, s, 1:2], LN_EPS, None, ALU.add).then_inc(var_ready, 1)
                dve.wait_ge(std_ready, s + 1)
                V.reciprocal(spread[:, s, 1:2], spread[:, s, 0:1]).then_inc(rstd_ready, 1)
                dve.wait_ge(rstd_ready, s + 1)
                for i in range(4):
                    z = z_rows[s][:, i, :]
                    V.scalar_tensor_tensor(z, z, moments[:, s, 0:1], ln_gb[:, 0, i * S:(i + 1) * S], ALU.subtract,
                                           ALU.mult).then_inc(centred, 1)
                    dve.wait_ge(centred, 4 * s + i + 1)
                    V.scalar_tensor_tensor(z, z, spread[:, s, 1:2], ln_gb[:, 1, i * S:(i + 1) * S], ALU.mult, ALU.add
                                           ).then_inc(normed, 1)

            def column_group(g):
                for s in range(2):
                    add_residual(g, s)
                for k in range(KT):
                    low_chunk(g + 1, k)
                for s in range(2, NB):
                    add_residual(g, s)

            column_group(0)
            with dve.Fori(1, 3) as g:
                column_group(g)
            dve.wait_ge(ln_landed, 32)
            for s in range(NB):
                add_residual(3, s)
                normalise(s)

        @block.tensor
        def _(pe):
            mm = nc.tensor.matmul

            def multiply(turn, quarters, act_hi, act_lo, bank, k_tiles=KT, before_tile=None):
                for s in quarters:
                    pe.wait_ge(lo_ready, 4 * turn + s + 1)
                    for kk in range(4):
                        k = (4 * s + kk) % k_tiles
                        if before_tile:
                            before_tile(k)
                        mm(bank, w_hi[:, s, kk, :], act_hi[:, k, :], start=(k == 0), stop=False)
                        mm(bank, w_hi[:, s, kk, :], act_lo[:, k, :], start=False, stop=False)
                        last = mm(bank, w_lo[:, s, kk, :], act_hi[:, k, :], start=False, stop=(k == k_tiles - 1))
                    last.then_inc(multiplied, 1)

            for n in range(8):
                pe.wait_ge(lo_ready, n + 1)
                bank = (bank_a, bank_b)[n % 2][:, :]
                for kk in range(4):
                    k = 4 * (n // 2) + kk
                    if n % 2 == 0:
                        pe.wait_ge(xt_lo_ready, k + 1)
                    mm(bank, w_hi[:, n % 4, kk, :], xt_hi[:, k, :], start=(k == 0), stop=False)
                    mm(bank, w_hi[:, n % 4, kk, :], xt_lo[:, k, :], start=False, stop=False)
                    last = mm(bank, w_lo[:, n % 4, kk, :], xt_hi[:, k, :], start=False, stop=(k == KT - 1))
                last.then_inc(multiplied, 1)
            pe.wait_ge(table_landed, 32)
            pe.wait_ge(table_filled, 2)
            mm(bank_o[0:HEADS, 0:SPAN], bias_table[:, :], buckets[:, :], start=True, stop=True).then_inc(rows_done, 1)

            pe.wait_ge(a_free, 1)
            multiply(T_VK + KVT, range(4), xt_hi, xt_lo, bank_a[:, :])
            pe.wait_ge(ident_ready, 1)
            pe.wait_ge(b_free, 1)
            for t in range(KVT):
                for b in range(NB):
                    ins = nc.tensor.transpose(bank_t[:, t, b * P:(b + 1) * P], v_t[:, t, b * P:(b + 1) * P], ident[:, :])
                ins.then_inc(v_turned, 1)
            multiply(T_VK + KVT + 1, range(4), xt_hi, xt_lo, bank_b[:, :])

            with pe.Fori(0, AT) as j:
                pe.wait_ge(a_free, A_QG + j)
                multiply(T_QG + 2 * j, range(4), xt_hi, xt_lo, bank_a[:, :])
                pe.wait_ge(b_free, B_QG + j)
                multiply(T_QG + 1 + 2 * j, range(4), xt_hi, xt_lo, bank_b[:, :])

            def score(i, first):
                pe.wait_ge(qk_staged, 3 * i + 3)
                if not first:
                    pe.wait_ge(biased, i)
                for t in range(2):
                    for half in range(2):
                        rows = slice(64 * half, 64 * half + 64)
                        ins = mm(scores[:, 2 * half + t, :], q_item[rows, t * P:(t + 1) * P], k_item[rows, :],
                                 start=True, stop=True)
                        if t == 1:
                            ins.then_inc(scores_done, 1)

            def weigh_values(i, first):
                pe.wait_ge(turned_saved, 2 * i + 2)
                pe.wait_ge(v_staged, 2 * i + 2)
                if not first:
                    pe.wait_ge(attn_gated, i)
                for w in range(2):
                    for half in range(2):
                        ins = mm(bank_o[64 * half:64 * half + 64, 0:2 * P], v_item[:, w, :],
                                 probs_t[:, w, 2 * P * half:2 * P * half + 2 * P],
                                 start=(w == 0), stop=(w == 1))
                ins.then_inc(pv_done, 1)

            def turn_probs(i):
                pe.wait_ge(probs_ready, i + 1)
                for w in range(2):
                    for h in range(GROUP):
                        ins = nc.tensor.transpose(bank_t[:, w, h * P:(h + 1) * P], probs[:, h, w * P:(w + 1) * P],
                                                  ident[:, :])
                    ins.then_inc(turned, 1)

            def item(i, second=False):
                score(i, False)
                pe.wait_ge(a_free, A_MA + i)
                multiply(T_MA + i, [0], xt_hi, xt_lo, bank_a[:, :])
                weigh_values(i - 1, second)
                multiply(T_MA + i, [1, 2, 3], xt_hi, xt_lo, bank_a[:, :])
                turn_probs(i)

            pe.wait_ge(v_saved, KVT)
            score(0, True)
            pe.wait_ge(a_free, A_MA)
            multiply(T_MA, range(4), xt_hi, xt_lo, bank_a[:, :])
            turn_probs(0)
            item(1, second=True)
            with pe.Fori(2, ITEMS) as i:
                item(i)
            multiply(T_X0, [0], xt_hi, xt_lo, bank_s[:, 0, :])
            weigh_values(ITEMS - 1, False)
            multiply(T_X0, [1, 2, 3], xt_hi, xt_lo, bank_s[:, 0, :])

            pe.wait_ge(ag_lo_ready, AT)
            with pe.Fori(0, KT // 2) as c:
                pe.wait_ge(b_free, B_AO + c)
                multiply(T_AO + c, [0, 1], ag_hi, ag_lo, bank_b[:, :], k_tiles=AT)
                pe.wait_ge(a_free, A_AO + c)
                multiply(T_AO + c, [2, 3], ag_hi, ag_lo, bank_a[:, :], k_tiles=AT)

            def recurrent_gates(c):
                pe.wait_ge(b_free, B_RN + c)
                multiply(T_RN + 2 * c, [0, 1, 2], xt_hi, xt_lo, bank_b[:, :])
                pe.wait_ge(gate_w_lo_ready, c + 1)
                pe.wait_ge(xc_lo_ready, c + 1)
                for n in range(2):
                    mm(bank_s[:, n, :], gate_w_hi[:, n, :], xc_hi[:, :], start=True, stop=False)
                    mm(bank_s[:, n, :], gate_w_hi[:, n, :], xc_lo[:, :], start=False, stop=False)
                    ins = mm(bank_s[:, n, :], gate_w_lo[:, n, :], xc_hi[:, :], start=False, stop=True)
                ins.then_inc(gates_done, 1)
                multiply(T_RN + 2 * c, [3], xt_hi, xt_lo, bank_b[:, :])

            with pe.Fori(0, KT - 1) as c:
                recurrent_gates(c)
                pe.wait_ge(a_free, A_RN + c)
                multiply(T_RN + 1 + 2 * c, range(4), xt_hi, xt_lo, bank_a[:, :])
            recurrent_gates(KT - 1)

            def branch_tile_ready(k):
                pe.wait_ge(hg_lo_ready, KT if k == KT - 1 else KT - 1)

            pe.wait_ge(a_free, A_MX)
            multiply(T_MX, range(4), xt_hi, xt_lo, bank_a[:, :])
            pe.wait_ge(b_free, B_MX)
            multiply(T_MX + 1, range(4), hg_hi, hg_lo, bank_b[:, :], before_tile=branch_tile_ready)
            with pe.Fori(1, KT) as c:
                pe.wait_ge(sig_mr_ready, c)
                multiply(T_MX + 2 * c, range(4), xt_hi, xt_lo, bank_a[:, :])
                pe.wait_ge(mixed_r_ready, c)
                multiply(T_MX + 1 + 2 * c, range(4), hg_hi, hg_lo, bank_b[:, :])

            def output_products(s, k):
                rows = slice(s * P, (s + 1) * P)
                mm(out_banks[s], hg_hi[:, k, rows], xt_hi[:, k, :], start=(k == 0), stop=False)
                mm(out_banks[s], hg_lo[:, k, rows], xt_hi[:, k, :], start=False, stop=False)
                return mm(out_banks[s], hg_hi[:, k, rows], xt_lo[:, k, :], start=False, stop=(k == KT - 1))

            def column_group(g, first=False):
                for pair in range(2):
                    if not first:
                        pe.wait_ge(z_ready, NB * g - NB + 2 * pair + 2)
                    for k in range(KT):
                        if pair == 0:
                            pe.wait_ge(chunk_lo_ready, KT * g + k + 1)
                            if first:
                                pe.wait_ge(mg_lo_ready, k + 1)
                        for s in (2 * pair, 2 * pair + 1):
                            last = output_products(s, k)
                        if pair == 1:
                            last.then_inc(wo_released, 1)
                    if pair == 0:
                        last.then_inc(rows_summed, 2)
                    else:
                        pe.wait_ge(wo_released, KT * g + KT)
                        pe.sem_inc(rows_summed, 2)

            column_group(0, first=True)
            with pe.Fori(1, 3) as g:
                column_group(g)
            for s in range(NB):
                pe.wait_ge(z_ready, NB * 2 + s + 1)
                for k in range(KT):
                    if s == 0:
                        pe.wait_ge(chunk_lo_ready, KT * 3 + k + 1)
                    last = output_products(s, k)
                last.then_inc(rows_summed, 1)


def bucket_row_constants():
    import math

    import numpy as np

    buckets, max_distance, window = 32, 128, 128
    exact = buckets // 2
    rows = np.zeros((buckets + 1, 3 * window), np.float32)
    for t in range(3 * window):
        n = 2 * window - 1 - t
        if not 0 <= n < window:
            b = buckets
        elif n < exact:
            b = n
        else:
            b = min(exact + int(math.log(n / exact) / math.log(max_distance / exact) * (buckets - exact)), buckets - 1)
        rows[b, t] = 1.0
    return rows


def kernel(x, w_in, conv_w, conv_b, w_r, b_r, w_i, b_i, lru_lambda, sinks, w_attn_out, w_rnn_out, w_out,
           ln_g, ln_b, rel_bias):
    import numpy as np
    import concourse.bacc as bacc
    from concourse.bass_utils import run_bass_kernel_spmd

    c = np.ascontiguousarray
    chan = np.concatenate([np.asarray(conv_w)[0], np.asarray(conv_b), np.asarray(b_r), np.asarray(b_i),
                           np.asarray(lru_lambda)])
    chan = c(chan.reshape(8, -1, P).transpose(2, 1, 0))
    arrays = {
        "x_t": c(np.asarray(x)[0].T), "x": c(x), "w_in": c(w_in), "chan": chan, "w_r": c(w_r), "w_i": c(w_i),
        "sinks": c(sinks), "w_attn_out": c(w_attn_out), "w_rnn_out": c(w_rnn_out), "w_out": c(w_out),
        "ln_g": c(ln_g), "ln_b": c(ln_b), "rel_bias": c(rel_bias), "bucket_rows": bucket_row_constants(),
    }
    nc = bacc.Bacc("TRN2", target_bir_lowering=False, num_devices=1)
    args = [nc.dram_tensor(name, a.shape, mybir.dt.from_np(a.dtype), kind="ExternalInput").ap()
            for name, a in arrays.items()]
    out = nc.dram_tensor("out", tuple(np.asarray(x).shape), F32, kind="ExternalOutput").ap()
    hybrid_layer(nc, *args, out)
    r = run_bass_kernel_spmd(nc, [arrays], core_ids=[0])
    return r.results[0]["out"]
```

```python
from contextlib import ExitStack

import concourse.bass as bass
from concourse import mybir

F32 = mybir.dt.float32
F32R = mybir.dt.float32r
ALU = mybir.AluOpType
ACT = mybir.ActivationFunctionType
AX = mybir.AxisListType

P = 128
NEG_INF = -1e30
LN_EPS = 1e-5
LRU_C = 8.0
DEPTH = 1
ALPHA = (2.0 * DEPTH) ** 0.25


def hybrid_layer(nc, x_t, x, w_in, chan, w_r, w_i, sinks, w_attn_out, w_rnn_out, w_out,
                 ln_g, ln_b, rel_bias, bucket_rows, out):
    D, S = x_t.shape
    KT = D // P
    HEADS = sinks.shape[1]
    HD = w_attn_out.shape[1] // HEADS
    KV_HEADS = 4
    GROUP = HEADS // KV_HEADS
    NB = S // P
    AT = HEADS * HD // P
    KVT = KV_HEADS * HD // P
    ITEMS = NB * KV_HEADS
    assert GROUP == 4 and HD == 64 and S == 512 and KT == 16 and ITEMS == KT
    SCALE = HD ** -0.5
    BUCKETS = rel_bias.shape[0]
    SPAN = bucket_rows.shape[1]

    COL_Q = 0
    COL_K = COL_Q + AT * P
    COL_V = COL_K + KVT * P
    COL_GA = COL_V + KVT * P
    COL_X = COL_GA + AT * P
    COL_GR = COL_X + D
    COL_MA = COL_GR + D
    COL_MR = COL_MA + D

    T_VK = 0
    T_QG = T_VK + 2 * KVT
    T_MA = T_QG + 2 * AT
    T_X0 = T_MA + KT
    T_AO = T_X0 + 1
    T_RN = T_AO + KT // 2
    T_MX = T_RN + 2 * KT - 1
    T_WO = T_MX + 2 * KT
    A_QG = KVT
    A_MA = A_QG + AT
    A_AO = A_MA + KT // 2
    A_RN = A_AO + KT // 2
    A_MX = A_RN + KT - 1
    B_QG = KVT
    B_MA = B_QG + AT
    B_AO = B_MA + KT // 2
    B_RN = B_AO + KT // 2
    B_MX = B_RN + KT

    w_in_v = w_in[0].rearrange("(k p) n -> p k n", p=P)
    w_ao_v = w_attn_out[0].rearrange("(k p) n -> p k n", p=P)
    w_ro_v = w_rnn_out[0].rearrange("(k p) n -> p k n", p=P)
    w_out_v = w_out[0].rearrange("(k p) n -> p k n", p=P)
    w_r_v = w_r[0].rearrange("h i j -> i h j")
    w_i_v = w_i[0].rearrange("h i j -> i h j")
    x_t_v = x_t.rearrange("(k p) s -> p k s", p=P)
    x_v = x[0].rearrange("(b p) d -> p b d", p=P)
    out_v = out[0].rearrange("(b p) d -> p b d", p=P)
    ds = bass.ds
    WARM_UP = 9

    with ExitStack() as ctx:
        def sb(name, shape, dt=F32, where=ctx):
            return where.enter_context(nc.sbuf_tensor(name, shape, dt))

        def sem(name):
            return ctx.enter_context(nc.semaphore(name))

        def ps(name, shape):
            return ctx.enter_context(nc.psum_tensor(name, shape, F32))

        bias_rows_d = nc.dram_tensor("bias_rows", [HEADS, P, SPAN], F32, kind="Internal").ap()

        xt_hi = sb("xt_hi", [P, KT, S], F32R)
        xt_lo = sb("xt_lo", [P, KT, S], F32R)
        queries = ExitStack()
        q_stack = sb("q_stack", [P, NB, KV_HEADS, GROUP * P], F32R, where=queries)
        queries.close()
        merged = sb("merged", [P, KT, S])
        raw = sb("raw", [P, 2, 8, P])
        w_hi = sb("w_hi", [P, 4, 4, P], F32R)
        w_lo = sb("w_lo", [P, 4, 4, P], F32R)
        gate_raw = ExitStack()
        gate_w = sb("gate_w", [P, 2, P], where=gate_raw)
        gate_raw.close()
        stats = sb("stats", [P, NB, 4, 6])
        moments = sb("moments", [P, NB, 2])
        spread = sb("spread", [P, NB, 2])
        sb("pad_gate_raw", [P, 2 * P - 28 * NB])
        gate_w_hi = sb("gate_w_hi", [P, 2, P], F32R)
        gate_w_lo = sb("gate_w_lo", [P, 2, P], F32R)
        chan_sb = sb("chan_sb", [P, KT, 8])
        exp_scale = sb("exp_scale", [P, KT])
        tanh_scale = sb("tanh_scale", [P, KT])

        early = ExitStack()
        k_hi = sb("k_hi", [P, KV_HEADS, S], F32R, where=early)
        k_lo = sb("k_lo", [P, KV_HEADS, S], F32R, where=early)
        bias = sb("bias", [P, HEADS, 2 * P], where=early)
        g_attn = sb("g_attn", [P, NB, AT * P], where=early)
        v_t = sb("v_t", [P, KVT, S], where=early)
        sig_qg = sb("sig_qg", [P, S], where=early)
        v_sb = sb("v_sb", [P, NB, KV_HEADS * HD], where=early)
        sinks_sb = sb("sinks_sb", [P, HEADS], where=early)
        table_sb = sb("table_sb", [BUCKETS, HEADS], where=early)
        bias_table = sb("bias_table", [BUCKETS + 1, HEADS], where=early)
        buckets = sb("buckets", [BUCKETS + 1, SPAN], where=early)
        bias_rows = sb("bias_rows_sb", [HEADS, SPAN], where=early)
        sp = sb("sp", [P, 6, KT], where=early)
        sb("pad", [P, 1536 - 3 * HEADS - 2 * SPAN - 6 * KT], where=early)
        probs = sb("probs", [P, 2, GROUP, P], where=early)
        probs_t = sb("probs_t", [P, 2, GROUP * P], where=early)
        q_item = sb("q_item", [P, GROUP, P], F32R, where=early)
        k_hi_item = sb("k_hi_item", [P, 2 * P], F32R, where=early)
        k_lo_item = sb("k_lo_item", [P, 2 * P], F32R, where=early)
        v_item = sb("v_item", [P, 2, HD], where=early)
        ident = sb("ident", [P, P], where=early)
        masks = sb("masks", [P, 2, P], where=early)
        neg_sinks = sb("neg_sinks", [P, HEADS], where=early)
        small = sb("small", [P, 6, 4], where=early)
        early.close()

        hg_hi = sb("hg_hi", [P, KT, S], F32R)
        hg_lo = sb("hg_lo", [P, KT, S], F32R)
        middle = ExitStack()
        xc = sb("xc", [P, S], where=middle)
        rec_gate = sb("rec_gate", [P, S], where=middle)
        inp = sb("inp", [P, S], where=middle)
        decay = sb("decay", [P, S], where=middle)
        norm = sb("norm", [P, S], where=middle)
        hid = sb("hid", [P, S], where=middle)
        silu = sb("silu", [P, S], where=middle)
        gated = sb("gated", [P, S], where=middle)
        xc_hi = sb("xc_hi", [P, S], F32R, where=middle)
        xc_lo = sb("xc_lo", [P, S], F32R, where=middle)
        middle.close()
        late = ExitStack()
        EARLY = 8
        wo_early = sb("wo_early", [P, EARLY, S], where=late)
        late.close()
        ln_gb = sb("ln_gb", [P, 2, D])
        sig_mr = sb("sig_mr", [P, S])
        mixed_r = sb("mixed_r", [P, S])
        ag_hi, ag_lo = hg_hi[:, 0:AT, :], hg_hi[:, AT:2 * AT, :]

        def raw_quarter(turn, s):
            if isinstance(turn, int) and turn < KVT:
                return raw[:, s // 2, :, :].rearrange("p (k u) n -> p k u n", u=2)[:, :, s % 2, :]
            return raw[:, s // 2, 4 * (s % 2):4 * (s % 2) + 4, :]

        def chunk_source(g, k):
            if isinstance(g, int) and g == 0 and k < EARLY:
                return wo_early[:, k, :]
            return raw[:, k // 2 % 2, 4 * (k % 2):4 * (k % 2) + 4, :].rearrange("p k n -> p (k n)")

        def norm_pieces(s):
            cuts = [0, 512, 1024, 1536, 1792, D] if s == NB - 1 else [0, 512, 1024, 1536, D]
            return list(zip(cuts[:-1], cuts[1:]))

        bank_a = ps("bank_a", [P, S])
        bank_b = ps("bank_b", [P, S])
        bank_s = ps("bank_s", [P, 2, S])
        bank_t = ps("bank_t", [P, 2, S])
        bank_o = ps("bank_o", [P, S])
        scores = bank_s[:, :, :].rearrange("p a (h k) -> p (a h) k", h=2)
        out_banks = [bank_s[:, 0, :], bank_s[:, 1, :], bank_t[:, 0, :], bank_t[:, 1, :]]

        raw_landed = [sem("raw_landed0"), sem("raw_landed1")]
        hi_ready = sem("hi_ready")
        lo_ready = sem("lo_ready")
        multiplied = sem("multiplied")
        a_free = sem("a_free")
        b_free = sem("b_free")
        X_CUTS = [0, 1, 2, 4, 6, 8, 12, 16]
        x_landed = [sem(f"x_landed{i}") for i in range(len(X_CUTS) - 1)]
        xt_hi_ready = sem("xt_hi_ready")
        xt_lo_ready = sem("xt_lo_ready")
        chan_landed = sem("chan_landed")
        sinks_landed = sem("sinks_landed")
        table_landed = sem("table_landed")
        table_filled = sem("table_filled")
        sinks_ready = sem("sinks_ready")
        soft_step = sem("soft_step")
        soft_exp = sem("soft_exp")
        scales_ready = sem("scales_ready")
        rows_done = sem("rows_done")
        rows_copied = sem("rows_copied")
        rows_stored = sem("rows_stored")
        bias_landed = sem("bias_landed")
        ident_zero = sem("ident_zero")
        ident_ready = sem("ident_ready")
        k_hi_saved = sem("k_hi_saved")
        k_saved = sem("k_saved")
        q_hi_saved = sem("q_hi_saved")
        q_saved = sem("q_saved")
        first_landed = [sem("first_landed0"), sem("first_landed1")]
        warm_up = sem("warm_up")
        v_turned = sem("v_turned")
        v_saved = sem("v_saved")
        sig_qg_ready = sem("sig_qg_ready")
        qk_staged = sem("qk_staged")
        v_staged = sem("v_staged")
        scores_done = sem("scores_done")
        masks_set = sem("masks_set")
        masks_ready = sem("masks_ready")
        prev_biased = sem("prev_biased")
        combined = sem("combined")
        biased = sem("biased")
        row_max = sem("row_max")
        shift_ready = sem("shift_ready")
        sink_shifted = sem("sink_shifted")
        exp_done = sem("exp_done")
        denom_ready = sem("denom_ready")
        recip_ready = sem("recip_ready")
        probs_ready = sem("probs_ready")
        turned = sem("turned")
        turned_saved = sem("turned_saved")
        pv_done = sem("pv_done")
        attn_gated = sem("attn_gated")
        ag_hi_ready = sem("ag_hi_ready")
        ag_lo_ready = sem("ag_lo_ready")
        gate_w_landed = sem("gate_w_landed")
        conv_begun = sem("conv_begun")
        conv_tap = sem("conv_tap")
        gate_w_hi_ready = sem("gate_w_hi_ready")
        gate_w_lo_ready = sem("gate_w_lo_ready")
        xc_hi_ready = sem("xc_hi_ready")
        xc_lo_ready = sem("xc_lo_ready")
        gates_done = sem("gates_done")
        sig_r_ready = sem("sig_r_ready")
        sig_i_ready = sem("sig_i_ready")
        gated_x = sem("gated_x")
        decay_ready = sem("decay_ready")
        tanh_ready = sem("tanh_ready")
        decay_sq = sem("decay_sq")
        norm_sq = sem("norm_sq")
        norm_ready = sem("norm_ready")
        drive_ready = sem("drive_ready")
        scan_done = sem("scan_done")
        sig_gr_ready = sem("sig_gr_ready")
        branch_ready = sem("branch_ready")
        hg_hi_ready = sem("hg_hi_ready")
        hg_lo_ready = sem("hg_lo_ready")
        sig_mr_ready = sem("sig_mr_ready")
        mixed_r_ready = sem("mixed_r_ready")
        merged_ready = sem("merged_ready")
        mg_hi_ready = sem("mg_hi_ready")
        mg_lo_ready = sem("mg_lo_ready")
        chunk_hi_ready = sem("chunk_hi_ready")
        chunk_lo_ready = sem("chunk_lo_ready")
        early_landed = sem("early_landed")
        ln_landed = sem("ln_landed")
        res_landed = [sem(f"res_landed{s}") for s in range(NB)]
        wo_released = sem("wo_released")
        pair_summed = sem("pair_summed")
        rows_summed = sem("rows_summed")
        z_ready = sem("z_ready")
        stats_ready = sem("stats_ready")
        mom_ready = sem("mom_ready")
        var_ready = sem("var_ready")
        std_ready = sem("std_ready")
        rstd_ready = sem("rstd_ready")
        centred = sem("centred")
        normed = sem("normed")
        stored = sem("stored")

        block = ctx.enter_context(nc.Block())

        @block.sync
        def _(sp_eng):
            def load_half(turn, half, src):
                if not (isinstance(turn, int) and turn == 0):
                    sp_eng.wait_ge(lo_ready, 4 * turn + 2 * half - 2)
                shape = raw[:, half, :, :]
                if src.shape[1] != 8:
                    shape = shape.rearrange("p (k a) n -> p k (a n)", k=src.shape[1])
                sp_eng.dma_start(shape, src).then_inc(raw_landed[half], 16)

            def load_turn(turn, src_v, col):
                for half in range(2):
                    load_half(turn, half, src_v[:, 8 * half:8 * half + 8, ds(col, P)])

            def load_x(i):
                a, b = X_CUTS[i], X_CUTS[i + 1]
                sp_eng.dma_start(merged[:, a:b, :], x_t_v[:, a:b, :]).then_inc(x_landed[i], 16)

            def load_quarter(s, landed):
                k, column = 4 * (s // 2), COL_V + s % 2 * P
                sp_eng.dma_start(raw_quarter(0, s), w_in_v[:, k:k + 4, column:column + P]).then_inc(landed, 16)

            load_quarter(0, first_landed[0])
            load_x(1)
            load_x(2)
            load_quarter(1, raw_landed[0])
            load_quarter(2, first_landed[1])
            load_x(3)
            load_quarter(3, raw_landed[1])
            load_x(4)
            load_x(5)
            load_half(T_VK + 1, 0, w_in_v[:, 8:12, COL_V:COL_V + KVT * P])
            load_x(6)
            load_half(T_VK + 1, 1, w_in_v[:, 12:16, COL_V:COL_V + KVT * P])
            sp_eng.dma_start(table_sb[:, :], rel_bias).then_inc(table_landed, 16)
            sp_eng.dma_start(buckets[:, :], bucket_rows).then_inc(table_landed, 16)
            for u in range(KVT):
                load_turn(T_VK + KVT + u, w_in_v, COL_K + P * u)
            sp_eng.dma_start(chan_sb[:, :, :], chan).then_inc(chan_landed, 16)
            sp_eng.dma_start(sinks_sb[:, :], sinks[0].partition_broadcast(P)).then_inc(sinks_landed, 16)
            with sp_eng.Fori(0, AT) as j:
                load_turn(T_QG + 2 * j, w_in_v, COL_Q + P * j)
                load_turn(T_QG + 1 + 2 * j, w_in_v, COL_GA + P * j)
            with sp_eng.Fori(0, KT) as c:
                load_turn(T_MA + c, w_in_v, COL_MA + P * c)
            load_turn(T_X0, w_in_v, COL_X)
            with sp_eng.Fori(0, KT // 2) as c:
                for half in range(2):
                    load_half(T_AO + c, half, w_ao_v[:, :, ds(2 * P * c + P * half, P)])

            def load_gate_weights(c):
                sp_eng.wait_ge(multiplied, 4 * T_RN - 3 + 8 * c)
                sp_eng.dma_start(gate_w[:, 0:1, :], w_r_v[:, ds(c, 1), :]).then_inc(gate_w_landed, 16)
                sp_eng.dma_start(gate_w[:, 1:2, :], w_i_v[:, ds(c, 1), :]).then_inc(gate_w_landed, 16)

            with sp_eng.Fori(0, KT - 1) as c:
                load_turn(T_RN + 2 * c, w_in_v, COL_GR + P * c)
                load_gate_weights(c)
                load_turn(T_RN + 1 + 2 * c, w_in_v, COL_X + P + P * c)
            load_turn(T_RN + 2 * KT - 2, w_in_v, COL_GR + P * (KT - 1))
            load_gate_weights(KT - 1)
            with sp_eng.Fori(1, KT + 1) as n:
                load_turn(T_MX - 2 + 2 * n, w_in_v, COL_MR - P + P * n)
                load_turn(T_MX - 1 + 2 * n, w_ro_v, P * n - P)
            def load_chunks(h, columns, ready, count):
                sp_eng.wait_ge(ready, count)
                sp_eng.dma_start(raw[:, h % 2, :, :].rearrange("p (k a) n -> p k (a n)", k=2),
                                 w_out_v[:, 2 * h:2 * h + 2, columns]).then_inc(raw_landed[h % 2], 16)

            for h in range(EARLY // 2, EARLY // 2 + 2):
                load_chunks(h, slice(0, S), lo_ready, 4 * T_WO - 2 + 2 * (h % 2))
            for h in range(EARLY // 2 + 2, KT // 2):
                load_chunks(h, slice(0, S), chunk_lo_ready, 2 * h - 2)
            with sp_eng.Fori(1, 4) as g:
                for h in range(KT // 2):
                    load_chunks(h, ds(S * g, S), chunk_lo_ready, KT * g + 2 * h - 2)
            for s in range(NB):
                row = merged[:, 4 * s:4 * s + 4, :].rearrange("p a n -> p (a n)")
                pieces = norm_pieces(s) if s == NB - 1 else [(0, D)]
                for n, (a, b) in enumerate(pieces):
                    sp_eng.wait_ge(normed, 4 * s + (n + 1 if s == NB - 1 else 4))
                    sp_eng.dma_start(out_v[:, s, a:b], row[:, a:b]).then_inc(stored, 16)
            sp_eng.wait_ge(stored, 16 * (NB - 1 + len(norm_pieces(NB - 1))))

        @block.gpsimd
        def _(pool):
            nc.gpsimd.memset(ident[:, :], 0.0).then_inc(ident_zero, 1)
            pool.wait_ge(ident_zero, 1)
            nc.gpsimd.affine_select(out=ident[:, :], in_=ident[:, :], compare_op=ALU.not_equal, fill=1.0,
                                    base=0, pattern=[[-1, P]], channel_multiplier=1).then_inc(ident_ready, 1)
            nc.gpsimd.memset(masks[:, :, :], 1.0).then_inc(masks_set, 1)
            pool.wait_ge(masks_set, 1)
            nc.gpsimd.affine_select(out=masks[:, 0, :], in_=masks[:, 0, :], compare_op=ALU.is_ge, fill=0.0,
                                    base=-1, pattern=[[-1, P]], channel_multiplier=1).then_inc(masks_ready, 1)
            nc.gpsimd.affine_select(out=masks[:, 1, :], in_=masks[:, 1, :], compare_op=ALU.is_ge, fill=0.0,
                                    base=0, pattern=[[1, P]], channel_multiplier=-1).then_inc(masks_ready, 1)
            pool.wait_ge(rows_copied, 1)
            pool.dma_start(bias_rows_d, bias_rows[:, :].unsqueeze(1).broadcast_to([HEADS, P, SPAN])
                           ).then_inc(rows_stored, 16)
            pool.wait_ge(rows_stored, 16)
            pool.dma_start(bias[:, :, :], bass.AP(tensor=bias_rows_d.tensor, offset=P - 1,
                                                  ap=[[SPAN - 1, P], [P * SPAN, HEADS], [1, 2 * P]])
                           ).then_inc(bias_landed, 16)

            def stage(i, b, g, first_block, first):
                if first:
                    pool.wait_ge(q_saved, 2 * AT)
                    pool.wait_ge(k_saved, 4 * KVT)
                else:
                    pool.wait_ge(scores_done, i)
                nc.gpsimd.tensor_copy(q_item[:, :, :].rearrange("p h n -> p (h n)"),
                                      q_stack[:, :, :, :].rearrange("p b g n -> p (b g n)")[:, ds(GROUP * P * i, GROUP * P)]
                                      ).then_inc(qk_staged, 1)
                for keys, item in ((k_hi, k_hi_item), (k_lo, k_lo_item)):
                    keys = keys[:, :, :].rearrange("p g s -> p (g s)")
                    if first_block:
                        nc.gpsimd.tensor_copy(item[:, 0:P], keys[:, ds(S * g, P)]).then_inc(qk_staged, 1)
                        nc.gpsimd.tensor_copy(item[:, P:2 * P], keys[:, ds(S * g, P)]).then_inc(qk_staged, 1)
                    else:
                        nc.gpsimd.tensor_copy(item[:, :], keys[:, ds(S * g + P * b - P, 2 * P)]).then_inc(qk_staged, 2)
                if first:
                    pool.wait_ge(v_saved, KVT)
                else:
                    pool.wait_ge(pv_done, i)
                values = v_sb[:, :, :].rearrange("p b n -> p (b n)")
                row = KV_HEADS * HD
                if not first_block:
                    nc.gpsimd.tensor_copy(v_item[:, 0, :], values[:, ds(row * b + HD * g - row, HD)]).then_inc(v_staged, 1)
                nc.gpsimd.tensor_copy(v_item[:, 1, :], values[:, ds(row * b + HD * g, HD)]).then_inc(v_staged, 1)

            stage(0, 0, 0, True, True)
            with pool.Fori(1, KV_HEADS) as g:
                stage(g, 0, g, True, False)
            with pool.Fori(1, NB) as b:
                with pool.Fori(0, KV_HEADS) as g:
                    stage(4 * b + g, b, g, False, False)

            pool.wait_ge(hg_lo_ready, KT)
            for k in range(0, EARLY, 4):
                pool.dma_start(wo_early[:, k:k + 4, :], w_out_v[:, k:k + 4, 0:S]).then_inc(early_landed, 16)
            pool.wait_ge(chunk_lo_ready, EARLY)
            pool.dma_start(ln_gb[:, 0, :], ln_g.partition_broadcast(P)).then_inc(ln_landed, 16)
            pool.dma_start(ln_gb[:, 1, :], ln_b.partition_broadcast(P)).then_inc(ln_landed, 16)
            pool.wait_ge(mg_lo_ready, KT)
            for s in range(NB):
                pool.dma_start(merged[:, 4 * s:4 * s + 4, :].rearrange("p a n -> p (a n)"), x_v[:, s, :]
                               ).then_inc(res_landed[s], 16)

        @block.scalar
        def _(act):
            act.dma_start(merged[:, 0:1, :], x_t_v[:, 0:1, :]).then_inc(x_landed[0], 16)
            act.wait_ge(warm_up, 1)
            nc.scalar.activation(spread[:, 1, :], spread[:, 0, :], ACT.Copy)

            def high_parts(turn, quarters):
                for s in quarters:
                    if isinstance(turn, int) and turn == 0 and s % 2 == 0:
                        act.wait_ge(first_landed[s // 2], 16)
                    elif s % 2 == 0 or isinstance(turn, int) and turn == 0:
                        act.wait_ge(raw_landed[s // 2], 16 * turn + 16)
                    if not (isinstance(turn, int) and turn == 0):
                        act.wait_ge(multiplied, 4 * turn + s - 3)
                    nc.scalar.activation(w_hi[:, s, :, :], raw_quarter(turn, s), ACT.Copy
                                         ).then_inc(hi_ready, 1)

            def high_chunk(g, k):
                if isinstance(g, int) and g == 0:
                    if k < EARLY:
                        act.wait_ge(early_landed, 32)
                    elif k % 2 == 0:
                        act.wait_ge(raw_landed[k // 2 % 2], 16 * (T_WO + 1 + (k - EARLY) // 4))
                    act.wait_ge(multiplied, 4 * (T_WO - 2) + k // 4 + 1)
                else:
                    if k % 2 == 0:
                        act.wait_ge(raw_landed[k // 2 % 2], 16 * (T_WO - 2 + k // 4 + 1) + 64 * g)
                    act.wait_ge(wo_released, KT * g - KT + k + 1)
                nc.scalar.activation(xt_hi[:, k, :], chunk_source(g, k), ACT.Copy).then_inc(chunk_hi_ready, 1)

            for k in range(KT):
                if k % 4 == 0:
                    high_parts(k // 8, [k // 2 % 4])
                if k in X_CUTS:
                    act.wait_ge(x_landed[X_CUTS.index(k)], 16)
                nc.scalar.activation(xt_hi[:, k, :], merged[:, k, :], ACT.Copy).then_inc(xt_hi_ready, 1)
                if k % 4 == 3:
                    high_parts(k // 8, [k // 2 % 4])
            high_parts(T_VK + KVT, range(4))
            for u, bank in ((0, bank_a), (1, bank_b)):
                high_parts(T_VK + KVT + u + 1, range(4))
                act.wait_ge(multiplied, 4 * (T_VK + KVT + u) + 4)
                for head in range(2):
                    for half in range(2):
                        nc.scalar.activation(k_hi[64 * half:64 * half + 64, 2 * u + head, :],
                                             bank[64 * head:64 * head + 64, :], ACT.Copy).then_inc(k_hi_saved, 1)
            act.wait_ge(soft_step, 2)
            nc.scalar.activation(sp[:, 1, :], sp[:, 1, :], ACT.Exp).then_inc(soft_exp, 1)

            with act.Fori(0, KV_HEADS) as g:
                for t in range(2):
                    high_parts(T_QG + 1 + 2 * t + 4 * g, range(4))
                    act.wait_ge(multiplied, 4 * T_QG + 4 + 8 * t + 16 * g)
                    for half in range(2):
                        rows, h = slice(64 * half, 64 * half + 64), 2 * half + t
                        nc.scalar.activation(q_stack[rows, :, ds(g, 1), h * P:(h + 1) * P],
                                             bank_a[rows, :].rearrange("p (b a n) -> p b a n", b=NB, a=1), ACT.Copy
                                             ).then_inc(q_hi_saved, 1)
                    high_parts(T_QG + 2 + 2 * t + 4 * g, range(4))
                    act.wait_ge(multiplied, 4 * T_QG + 8 + 8 * t + 16 * g)
                    nc.scalar.activation(sig_qg[:, :], bank_b[:, :], ACT.Sigmoid).then_inc(sig_qg_ready, 1)

            def attention_item(i, bank, free):
                act.wait_ge(sink_shifted, i + 1)
                nc.scalar.activation(small[:, 3, :], small[:, 2, :], ACT.Exp).then_inc(exp_done, 1)
                for h in range(GROUP):
                    nc.scalar.activation(probs[:, 0, h, :], probs[:, 0, h, :], ACT.Exp, bias=small[:, 1, h:h + 1],
                                         accum_out=small[:, 4, h:h + 1]).then_inc(exp_done, 1)
                high_parts(T_MA + 1 + i, range(4))
                act.wait_ge(multiplied, 4 * T_MA + 4 + 4 * i)
                nc.scalar.activation(merged[:, ds(i, 1), :], bank[:, :].unsqueeze(1), ACT.Sigmoid).then_inc(free, 1)

            with act.Fori(0, ITEMS // 2) as n:
                attention_item(2 * n, bank_a, a_free)
                attention_item(2 * n + 1, bank_b, b_free)

            def gated_high(k):
                nc.scalar.activation(ag_hi[:, k, :].rearrange("p (b n) -> p b n", b=NB),
                                     g_attn[:, :, k * P:(k + 1) * P], ACT.Copy).then_inc(ag_hi_ready, 1)

            act.wait_ge(attn_gated, ITEMS - 1)
            for k in range(AT - 2):
                gated_high(k)
            high_parts(T_AO, [0])
            act.wait_ge(attn_gated, ITEMS)
            for k in range(AT - 2, AT):
                gated_high(k)
            high_parts(T_AO, [1, 2, 3])

            def convolution_begin(c):
                if isinstance(c, int) and c == 0:
                    act.wait_ge(multiplied, 4 * T_X0 + 4)
                    bank = bank_s[:, 0, :]
                else:
                    act.wait_ge(multiplied, 4 * T_RN + 8 * c)
                    act.wait_ge(gated_x, c)
                    bank = bank_a[:, :]
                nc.scalar.activation(xc[:, :], bank, ACT.Identity, scale=chan_sb[:, ds(c, 1), 3],
                                     bias=chan_sb[:, ds(c, 1), 4]).then_inc(conv_begun, 1)

            def gate_operands_high(c):
                act.wait_ge(gate_w_landed, 32 * c + 32)
                nc.scalar.activation(gate_w_hi[:, :, :], gate_w[:, :, :], ACT.Copy).then_inc(gate_w_hi_ready, 1)
                act.wait_ge(conv_tap, 3 * c + 3)
                nc.scalar.activation(xc_hi[:, :], xc[:, :], ACT.Copy).then_inc(xc_hi_ready, 1)

            def gate_sigmoids(c):
                act.wait_ge(gates_done, c + 1)
                nc.scalar.activation(rec_gate[:, :], bank_s[:, 0, :], ACT.Sigmoid, bias=chan_sb[:, ds(c, 1), 5]
                                     ).then_inc(sig_r_ready, 1)
                nc.scalar.activation(inp[:, :], bank_s[:, 1, :], ACT.Sigmoid, bias=chan_sb[:, ds(c, 1), 6]
                                     ).then_inc(sig_i_ready, 1)

            def decays(c):
                act.wait_ge(sig_r_ready, c + 1)
                nc.scalar.activation(decay[:, :], rec_gate[:, :], ACT.Exp, scale=exp_scale[:, ds(c, 1)]
                                     ).then_inc(decay_ready, 1)
                nc.scalar.activation(norm[:, :], rec_gate[:, :], ACT.Tanh, scale=tanh_scale[:, ds(c, 1)]
                                     ).then_inc(tanh_ready, 1)

            def norm_root(c):
                act.wait_ge(norm_sq, c + 1)
                nc.scalar.activation(norm[:, :], norm[:, :], ACT.Sqrt).then_inc(norm_ready, 1)

            def branch_high(c):
                act.wait_ge(branch_ready, c + 1)
                nc.scalar.activation(hg_hi[:, ds(c, 1), :], gated[:, :].unsqueeze(1), ACT.Copy).then_inc(hg_hi_ready, 1)

            def recurrent_gates(c, first=False):
                gate_operands_high(c)
                high_parts(T_RN + 1 + 2 * c, [0, 1])
                if not first:
                    branch_high(c - 1)
                high_parts(T_RN + 1 + 2 * c, [2])
                gate_sigmoids(c)
                high_parts(T_RN + 1 + 2 * c, [3])
                act.wait_ge(multiplied, 4 * T_RN + 4 + 8 * c)
                nc.scalar.activation(silu[:, :], bank_b[:, :], ACT.Sigmoid).then_inc(sig_gr_ready, 1)

            def recurrent_decay(c):
                high_parts(T_RN + 2 + 2 * c, [0])
                decays(c)
                high_parts(T_RN + 2 + 2 * c, [1, 2])
                norm_root(c)
                high_parts(T_RN + 2 + 2 * c, [3])

            act.wait_ge(chan_landed, 16)
            act.wait_ge(scales_ready, 2)
            convolution_begin(0)
            with act.Fori(0, KT // 2) as c:
                high_parts(T_AO + 1 + c, range(4))
            recurrent_gates(0, first=True)
            recurrent_decay(0)
            convolution_begin(1)
            with act.Fori(1, KT - 1) as c:
                recurrent_gates(c)
                recurrent_decay(c)
                convolution_begin(c + 1)
            recurrent_gates(KT - 1)

            def merge_tile(c, first=False, last=False):
                if first:
                    recurrent_decay(KT - 1)
                    branch_high(KT - 1)
                else:
                    for s in range(4):
                        high_parts(T_MX + 1 + 2 * c, [s])
                        if last:
                            high_chunk(0, 2 * s)
                            high_chunk(0, 2 * s + 1)
                    act.wait_ge(mixed_r_ready, c)
                act.wait_ge(multiplied, 4 * T_MX + 4 + 8 * c)
                nc.scalar.activation(sig_mr[:, :], bank_a[:, :], ACT.Sigmoid).then_inc(sig_mr_ready, 1)
                if not last:
                    high_parts(T_MX + 2 + 2 * c, range(4))

            merge_tile(0, first=True)
            with act.Fori(1, KT - 1) as c:
                merge_tile(c)
            merge_tile(KT - 1, last=True)

            def merged_high(k):
                act.wait_ge(multiplied, 4 * (T_WO - 1) + k // 4 + 1)
                act.wait_ge(merged_ready, k + 1)
                nc.scalar.activation(hg_hi[:, k, :], merged[:, k, :], ACT.Copy).then_inc(mg_hi_ready, 1)

            for k in range(8):
                high_chunk(0, 8 + k)
                merged_high(k)
            for k in range(8, KT):
                merged_high(k)
            with act.Fori(1, 4) as g:
                for k in range(KT):
                    high_chunk(g, k)
            for s in range(NB):
                act.wait_ge(var_ready, s + 1)
                nc.scalar.activation(spread[:, s, 0:1], moments[:, s, 1:2], ACT.Sqrt).then_inc(std_ready, 1)

        @block.vector
        def _(dve):
            V = nc.vector

            def low_parts(turn, quarters):
                for s in quarters:
                    dve.wait_ge(hi_ready, 4 * turn + s + 1)
                    V.tensor_tensor(w_lo[:, s, :, :], raw_quarter(turn, s), w_hi[:, s, :, :], ALU.subtract
                                    ).then_inc(lo_ready, 1)

            def low_chunk(g, k):
                dve.wait_ge(chunk_hi_ready, KT * g + k + 1)
                V.tensor_tensor(xt_lo[:, k, :], chunk_source(g, k), xt_hi[:, k, :], ALU.subtract
                                ).then_inc(chunk_lo_ready, 1)

            V.memset(spread[:, 0, :], 0.0).then_inc(warm_up, 1)
            V.memset(bias_table[BUCKETS:BUCKETS + 1, :], NEG_INF).then_inc(table_filled, 1)
            for k in range(KT):
                if k % 4 == 0:
                    low_parts(k // 8, [k // 2 % 4])
                dve.wait_ge(xt_hi_ready, k + 1)
                V.tensor_tensor(xt_lo[:, k, :], merged[:, k, :], xt_hi[:, k, :], ALU.subtract).then_inc(xt_lo_ready, 1)
                if k % 4 == 3:
                    low_parts(k // 8, [k // 2 % 4])
            dve.wait_ge(table_landed, 32)
            V.tensor_copy(bias_table[0:BUCKETS, :].rearrange("p (g h t) -> p g h t", t=2, h=2),
                          table_sb[:, :].rearrange("p (g t h) -> p g h t", t=2, h=2)).then_inc(table_filled, 1)


            low_parts(T_VK + KVT, [0, 1])
            dve.wait_ge(multiplied, 7)
            V.tensor_copy(v_t[:, 0, :], bank_a[:, :]).then_inc(a_free, 1)
            low_parts(T_VK + KVT, [2, 3])
            dve.wait_ge(multiplied, 8)
            V.tensor_copy(v_t[:, 1, :], bank_b[:, :]).then_inc(b_free, 1)
            dve.wait_ge(rows_done, 1)
            V.tensor_copy(bias_rows[:, :], bank_o[0:HEADS, 0:SPAN]).then_inc(rows_copied, 1)

            def save_keys(u, bank, free):
                for head in range(2):
                    dve.wait_ge(k_hi_saved, 4 * u + 2 * head + 2)
                    rows = slice(64 * head, 64 * head + 64)
                    for half in range(2):
                        V.tensor_tensor(k_lo[64 * half:64 * half + 64, 2 * u + head, :], bank[rows, :],
                                        k_hi[rows, 2 * u + head, :], ALU.subtract).then_inc(k_saved, 1)
                dve.wait_ge(k_saved, 4 * (u + 1))
                dve.sem_inc(free, 1)

            low_parts(T_VK + KVT + 1, range(4))
            save_keys(0, bank_a, a_free)
            for t in range(KVT):
                dve.wait_ge(v_turned, t + 1)
                V.tensor_copy(v_sb[:, :, t * P:(t + 1) * P], bank_t[:, t, :].rearrange("p (b n) -> p b n", b=NB)
                              ).then_inc(v_saved, 1)
            low_parts(T_QG, range(4))
            save_keys(1, bank_b, b_free)

            steps = 0

            def then_next(ins):
                nonlocal steps
                steps += 1
                ins.then_inc(soft_step, 1)
                dve.wait_ge(soft_step, steps)

            lam, negated, e, z, z2, acc = chan_sb[:, :, 7], sp[:, 0, :], sp[:, 1, :], sp[:, 2, :], sp[:, 3, :], sp[:, 4, :]
            dve.wait_ge(chan_landed, 16)
            then_next(V.tensor_scalar(negated, lam, -1.0, None, ALU.mult))
            then_next(V.tensor_tensor(e, negated, lam, ALU.min))
            dve.wait_ge(soft_exp, 1)
            then_next(V.tensor_scalar(z, e, 2.0, None, ALU.add))
            then_next(V.reciprocal(acc, z))
            then_next(V.tensor_tensor(z, e, acc, ALU.mult))
            then_next(V.tensor_tensor(z2, z, z, ALU.mult))
            then_next(V.tensor_scalar(acc, z2, 1.0 / 17, None, ALU.mult))
            for n in (15, 13, 11, 9, 7, 5, 3):
                then_next(V.scalar_tensor_tensor(acc, acc, 1.0 / n, z2, ALU.add, ALU.mult))
            then_next(V.scalar_tensor_tensor(acc, acc, 1.0, z, ALU.add, ALU.mult))
            then_next(V.tensor_scalar(negated, negated, 0.0, None, ALU.max))
            then_next(V.scalar_tensor_tensor(acc, acc, 2.0, negated, ALU.mult, ALU.add))
            V.tensor_scalar(exp_scale[:, :], acc, -LRU_C, None, ALU.mult).then_inc(scales_ready, 1)
            V.tensor_scalar(tanh_scale[:, :], acc, LRU_C, None, ALU.mult).then_inc(scales_ready, 1)
            dve.wait_ge(sinks_landed, 16)
            V.tensor_scalar(neg_sinks[:, :].rearrange("p (g h t) -> p g h t", t=2, h=2),
                            sinks_sb[:, :].rearrange("p (g t h) -> p g h t", t=2, h=2), -1.0, None, ALU.mult).then_inc(sinks_ready, 1)


            with dve.Fori(0, KV_HEADS) as g:
                for t in range(2):
                    low_parts(T_QG + 1 + 2 * t + 4 * g, range(4))
                    for half in range(2):
                        dve.wait_ge(q_hi_saved, 4 * g + 2 * t + half + 1)
                        rows, others, h = slice(64 * half, 64 * half + 64), slice(64 - 64 * half, 128 - 64 * half), 2 * half + t
                        V.tensor_tensor(q_stack[others, :, ds(g, 1), h * P:(h + 1) * P],
                                        bank_a[rows, :].rearrange("p (b a n) -> p b a n", b=NB, a=1),
                                        q_stack[rows, :, ds(g, 1), h * P:(h + 1) * P], ALU.subtract).then_inc(q_saved, 1)
                    dve.wait_ge(q_saved, 4 * g + 2 * t + 2)
                    dve.sem_inc(a_free, 1)
                    low_parts(T_QG + 2 + 2 * t + 4 * g, range(4))
                    dve.wait_ge(sig_qg_ready, 2 * g + t + 1)
                    V.tensor_tensor(g_attn[:, :, ds(2 * P * g + P * t, P)], bank_b[:, :].rearrange("p (b n) -> p b n", b=NB),
                                    sig_qg[:, :].rearrange("p (b n) -> p b n", b=NB), ALU.mult).then_inc(b_free, 1)

            def gate_item(i):
                dve.wait_ge(pv_done, i + 1)
                place = g_attn[:, :, :].rearrange("p b n -> p (b n)")[:, ds(2 * P * i, 2 * P)]
                V.tensor_tensor(place, bank_o[:, 0:2 * P], place, ALU.mult).then_inc(attn_gated, 1)

            def attention_item(i, g, first_block, first):
                dve.wait_ge(scores_done, i + 1)
                if not first_block:
                    V.scalar_tensor_tensor(probs[:, 1, :, :], scores[:, :, 0:P], SCALE, bias[:, ds(GROUP * g, GROUP), 0:P],
                                           ALU.mult, ALU.add).then_inc(prev_biased, 1)
                V.scalar_tensor_tensor(probs[:, 0, :, :], scores[:, :, P:2 * P], SCALE, bias[:, ds(GROUP * g, GROUP), P:2 * P],
                                       ALU.mult, ALU.add).then_inc(biased, 1)
                dve.wait_ge(biased, i + 1)
                if not first_block:
                    dve.wait_ge(prev_biased, i - KV_HEADS + 1)
                    V.tensor_tensor(probs[:, 0, :, :], probs[:, 0, :, :], probs[:, 1, :, :], ALU.max).then_inc(combined, 1)
                    dve.wait_ge(combined, i - KV_HEADS + 1)
                V.tensor_reduce(small[:, 0, :], probs[:, 0, :, :], AX.X, ALU.max).then_inc(row_max, 1)
                dve.wait_ge(row_max, i + 1)
                V.scalar_tensor_tensor(small[:, 1, :], small[:, 0, :], -1.0, neg_sinks[:, ds(GROUP * g, GROUP)],
                                       ALU.mult, ALU.min).then_inc(shift_ready, 1)
                dve.wait_ge(shift_ready, i + 1)
                V.tensor_tensor(small[:, 2, :], small[:, 1, :], neg_sinks[:, ds(GROUP * g, GROUP)], ALU.subtract
                                ).then_inc(sink_shifted, 1)
                low_parts(T_MA + 1 + i, [0])
                if not first:
                    gate_item(i - 1)
                low_parts(T_MA + 1 + i, [1])
                dve.wait_ge(exp_done, 5 * i + 5)
                V.tensor_tensor(small[:, 4, :], small[:, 4, :], small[:, 3, :], ALU.add).then_inc(denom_ready, 1)
                dve.wait_ge(denom_ready, i + 1)
                V.reciprocal(small[:, 5, :], small[:, 4, :]).then_inc(recip_ready, 1)
                dve.wait_ge(recip_ready, i + 1)
                V.tensor_tensor(probs[:, 0, :, :], probs[:, 0, :, :],
                                small[:, 5, :].unsqueeze(2).broadcast_to([P, GROUP, P]), ALU.mult
                                ).then_inc(probs_ready, 1)
                low_parts(T_MA + 1 + i, [2, 3])
                dve.wait_ge(turned, i + 1)
                for w in (1,) if first_block else (0, 1):
                    V.tensor_tensor(probs_t[:, w, :].rearrange("p (h q) -> p h q", h=GROUP),
                                    bank_t[:, 0, :].rearrange("p (h q) -> p h q", h=GROUP),
                                    masks[:, w, :].unsqueeze(1).broadcast_to([P, GROUP, P]), ALU.mult
                                    ).then_inc(turned_saved, 1)

            dve.wait_ge(bias_landed, 16)
            dve.wait_ge(sinks_ready, 1)
            dve.wait_ge(masks_ready, 2)
            attention_item(0, 0, True, True)
            with dve.Fori(1, KV_HEADS) as g:
                attention_item(g, g, True, False)
            with dve.Fori(1, NB) as b:
                with dve.Fori(0, KV_HEADS) as g:
                    attention_item(4 * b + g, g, False, False)

            def gated_low(k):
                dve.wait_ge(ag_hi_ready, k + 1)
                V.tensor_tensor(ag_lo[:, k, :].rearrange("p (b n) -> p b n", b=NB), g_attn[:, :, k * P:(k + 1) * P],
                                ag_hi[:, k, :].rearrange("p (b n) -> p b n", b=NB), ALU.subtract).then_inc(ag_lo_ready, 1)

            def convolution_taps(c):
                dve.wait_ge(conv_begun, c + 1)
                first = isinstance(c, int) and c == 0
                bank = bank_s[:, 0, :] if first else bank_a[:, :]
                for tap in range(3):
                    back = tap + 1
                    if tap:
                        dve.wait_ge(conv_tap, 3 * c + tap)
                    V.scalar_tensor_tensor(xc[:, back:S], bank[:, 0:S - back], chan_sb[:, ds(c, 1), 3 - back],
                                           xc[:, back:S], ALU.mult, ALU.add).then_inc(conv_tap, 1)
                if not first:
                    dve.wait_ge(conv_tap, 3 * c + 3)
                    dve.sem_inc(a_free, 1)

            for k in range(AT - 2):
                gated_low(k)
            low_parts(T_AO, [0])
            gate_item(ITEMS - 1)
            for k in range(AT - 2, AT):
                gated_low(k)
            low_parts(T_AO, [1, 2, 3])
            convolution_taps(0)
            dve.wait_ge(a_free, A_AO)
            dve.wait_ge(b_free, B_AO)
            with dve.Fori(0, KT // 2) as c:
                for bank, free, half in ((bank_b, b_free, 0), (bank_a, a_free, 1)):
                    low_parts(T_AO + 1 + c, [2 * half, 2 * half + 1])
                    dve.wait_ge(multiplied, 4 * T_AO + 2 + 2 * half + 4 * c)
                    V.tensor_tensor(merged[:, ds(2 * c + half, 1), :], bank[:, :].unsqueeze(1),
                                    merged[:, ds(2 * c + half, 1), :], ALU.mult).then_inc(free, 1)

            def drive_input(c):
                dve.wait_ge(sig_i_ready, c + 1)
                V.tensor_tensor(inp[:, :], inp[:, :], xc[:, :], ALU.mult).then_inc(gated_x, 1)

            def norm_square(c):
                dve.wait_ge(decay_ready, c + 1)
                V.tensor_tensor(hid[:, :], decay[:, :], decay[:, :], ALU.mult).then_inc(decay_sq, 1)
                dve.wait_ge(decay_sq, c + 1)
                dve.wait_ge(tanh_ready, c + 1)
                V.scalar_tensor_tensor(norm[:, :], hid[:, :], 1.0, norm[:, :], ALU.add, ALU.mult).then_inc(norm_sq, 1)

            def recurrence(c):
                dve.wait_ge(norm_ready, c + 1)
                dve.wait_ge(gated_x, c + 1)
                V.tensor_tensor(inp[:, :], inp[:, :], norm[:, :], ALU.mult).then_inc(drive_ready, 1)
                dve.wait_ge(drive_ready, c + 1)
                V.tensor_tensor_scan(hid[:, :], decay[:, :], inp[:, :], 0.0, ALU.mult, ALU.add).then_inc(scan_done, 1)
                dve.wait_ge(scan_done, c + 1)
                dve.wait_ge(b_free, B_RN + 1 + c)
                V.tensor_tensor(gated[:, :], hid[:, :], silu[:, :], ALU.mult).then_inc(branch_ready, 1)

            def branch_low(c):
                dve.wait_ge(hg_hi_ready, c + 1)
                V.tensor_tensor(hg_lo[:, ds(c, 1), :], gated[:, :].unsqueeze(1), hg_hi[:, ds(c, 1), :], ALU.subtract
                                ).then_inc(hg_lo_ready, 1)

            def recurrent_gates(c, first=False):
                dve.wait_ge(gate_w_hi_ready, c + 1)
                V.tensor_tensor(gate_w_lo[:, :, :], gate_w[:, :, :], gate_w_hi[:, :, :], ALU.subtract
                                ).then_inc(gate_w_lo_ready, 1)
                dve.wait_ge(xc_hi_ready, c + 1)
                V.tensor_tensor(xc_lo[:, :], xc[:, :], xc_hi[:, :], ALU.subtract).then_inc(xc_lo_ready, 1)
                low_parts(T_RN + 1 + 2 * c, [0])
                if not first:
                    recurrence(c - 1)
                low_parts(T_RN + 1 + 2 * c, [1])
                if not first:
                    branch_low(c - 1)
                low_parts(T_RN + 1 + 2 * c, [2, 3])
                dve.wait_ge(sig_gr_ready, c + 1)
                V.tensor_tensor(silu[:, :], bank_b[:, :], silu[:, :], ALU.mult).then_inc(b_free, 1)
                drive_input(c)

            def recurrent_decay(c):
                low_parts(T_RN + 2 + 2 * c, [0, 1])
                norm_square(c)
                low_parts(T_RN + 2 + 2 * c, [2, 3])
                convolution_taps(c + 1)

            recurrent_gates(0, first=True)
            recurrent_decay(0)
            with dve.Fori(1, KT - 1) as c:
                recurrent_gates(c)
                recurrent_decay(c)
            recurrent_gates(KT - 1)

            def add_branches(c):
                dve.wait_ge(sig_mr_ready, c + 1)
                dve.wait_ge(multiplied, 4 * T_MX + 8 + 8 * c)
                V.tensor_tensor(mixed_r[:, :], bank_b[:, :], sig_mr[:, :], ALU.mult).then_inc(mixed_r_ready, 1)
                dve.wait_ge(mixed_r_ready, c + 1)
                V.tensor_tensor(merged[:, ds(c, 1), :], merged[:, ds(c, 1), :], mixed_r[:, :].unsqueeze(1), ALU.add
                                ).then_inc(merged_ready, 1)

            low_parts(T_MX + 1, [0, 1])
            norm_square(KT - 1)
            low_parts(T_MX + 1, [2])
            recurrence(KT - 1)
            low_parts(T_MX + 1, [3])
            branch_low(KT - 1)
            low_parts(T_MX + 2, range(4))
            add_branches(0)
            with dve.Fori(1, KT - 1) as c:
                low_parts(T_MX + 1 + 2 * c, range(4))
                low_parts(T_MX + 2 + 2 * c, range(4))
                add_branches(c)
            for s in range(4):
                low_parts(T_WO - 1, [s])
                low_chunk(0, 2 * s)
                low_chunk(0, 2 * s + 1)

            def merged_low(k):
                dve.wait_ge(mg_hi_ready, k + 1)
                V.tensor_tensor(hg_lo[:, k, :], merged[:, k, :], hg_hi[:, k, :], ALU.subtract).then_inc(mg_lo_ready, 1)

            for k in range(8):
                low_chunk(0, 8 + k)
                merged_low(k)
            add_branches(KT - 1)
            for k in range(8, KT):
                merged_low(k)

            def add_residual(g, s):
                if isinstance(g, int) and g == 0:
                    dve.wait_ge(res_landed[s], 16)
                if isinstance(g, int) and g == 3:
                    dve.wait_ge(rows_summed, s + 1)
                elif s < 2:
                    dve.wait_ge(pair_summed, g + 1)
                else:
                    dve.wait_ge(wo_released, KT * g + KT)
                z = merged[:, ds(4 * s + g, 1), :]
                V.scalar_tensor_tensor(z, z, ALPHA, out_banks[s].unsqueeze(1), ALU.mult, ALU.add).then_inc(z_ready, 1)
                dve.wait_ge(z_ready, NB * g + s + 1)
                V.bn_stats(stats[:, s, ds(g, 1), :].rearrange("p a n -> p (a n)"), z.rearrange("p a n -> p (a n)")
                           ).then_inc(stats_ready, 1)

            def normalise(s):
                dve.wait_ge(stats_ready, NB * 3 + s + 1)
                V.bn_aggr(moments[:, s, :], stats[:, s, :, :].rearrange("p a n -> p (a n)")).then_inc(mom_ready, 1)
                dve.wait_ge(mom_ready, s + 1)
                V.tensor_scalar(moments[:, s, 1:2], moments[:, s, 1:2], LN_EPS, None, ALU.add).then_inc(var_ready, 1)
                dve.wait_ge(std_ready, s + 1)
                V.reciprocal(spread[:, s, 1:2], spread[:, s, 0:1]).then_inc(rstd_ready, 1)
                dve.wait_ge(rstd_ready, s + 1)
                row = merged[:, 4 * s:4 * s + 4, :].rearrange("p a n -> p (a n)")
                pieces = norm_pieces(s)

                def centre(n):
                    z = row[:, pieces[n][0]:pieces[n][1]]
                    V.scalar_tensor_tensor(z, z, moments[:, s, 0:1], ln_gb[:, 0, pieces[n][0]:pieces[n][1]], ALU.subtract,
                                           ALU.mult).then_inc(centred, 1)

                centre(0)
                for n, (a, b) in enumerate(pieces):
                    if n + 1 < len(pieces):
                        centre(n + 1)
                    dve.wait_ge(centred, 4 * s + n + 1)
                    V.scalar_tensor_tensor(row[:, a:b], row[:, a:b], spread[:, s, 1:2], ln_gb[:, 1, a:b], ALU.mult, ALU.add
                                           ).then_inc(normed, 1)

            def column_group(g):
                for s in range(2):
                    add_residual(g, s)
                for k in range(KT):
                    low_chunk(g + 1, k)
                for s in range(2, NB):
                    add_residual(g, s)

            column_group(0)
            with dve.Fori(1, 3) as g:
                column_group(g)
            dve.wait_ge(ln_landed, 32)
            for s in range(NB):
                add_residual(3, s)
                normalise(s)

        @block.tensor
        def _(pe):
            mm = nc.tensor.matmul

            def multiply(turn, quarters, act_hi, act_lo, bank, k_tiles=KT, before_tile=None):
                for s in quarters:
                    pe.wait_ge(lo_ready, 4 * turn + s + 1)
                    for kk in range(4):
                        k = (4 * s + kk) % k_tiles
                        if before_tile:
                            before_tile(k)
                        mm(bank, w_hi[:, s, kk, :], act_hi[:, k, :], start=(k == 0), stop=False)
                        mm(bank, w_hi[:, s, kk, :], act_lo[:, k, :], start=False, stop=False)
                        last = mm(bank, w_lo[:, s, kk, :], act_hi[:, k, :], start=False, stop=(k == k_tiles - 1))
                    last.then_inc(multiplied, 1)

            pe.wait_ge(ident_ready, 1)
            for _ in range(WARM_UP):
                mm(bank_o[:, 0:P], ident[:, :], ident[:, :], start=True, stop=True)

            for n in range(8):
                pe.wait_ge(lo_ready, n + 1)
                bank = (bank_a, bank_b)[n % 2][:, :]
                for kk in range(4):
                    k = 4 * (n // 2) + kk
                    if n % 2 == 0:
                        pe.wait_ge(xt_lo_ready, k + 1)
                    mm(bank, w_hi[:, n % 4, kk, :], xt_hi[:, k, :], start=(k == 0), stop=False)
                    mm(bank, w_hi[:, n % 4, kk, :], xt_lo[:, k, :], start=False, stop=False)
                    last = mm(bank, w_lo[:, n % 4, kk, :], xt_hi[:, k, :], start=False, stop=(k == KT - 1))
                last.then_inc(multiplied, 1)
            pe.wait_ge(table_landed, 32)
            pe.wait_ge(table_filled, 2)
            mm(bank_o[0:HEADS, 0:SPAN], bias_table[:, :], buckets[:, :], start=True, stop=True).then_inc(rows_done, 1)

            pe.wait_ge(a_free, 1)
            multiply(T_VK + KVT, range(4), xt_hi, xt_lo, bank_a[:, :])
            pe.wait_ge(ident_ready, 1)
            pe.wait_ge(b_free, 1)
            for t in range(KVT):
                for b in range(NB):
                    ins = nc.tensor.transpose(bank_t[:, t, b * P:(b + 1) * P], v_t[:, t, b * P:(b + 1) * P], ident[:, :])
                ins.then_inc(v_turned, 1)
            multiply(T_VK + KVT + 1, range(4), xt_hi, xt_lo, bank_b[:, :])

            with pe.Fori(0, AT) as j:
                pe.wait_ge(a_free, A_QG + j)
                multiply(T_QG + 2 * j, range(4), xt_hi, xt_lo, bank_a[:, :])
                pe.wait_ge(b_free, B_QG + j)
                multiply(T_QG + 1 + 2 * j, range(4), xt_hi, xt_lo, bank_b[:, :])

            def score(i, first):
                pe.wait_ge(qk_staged, 5 * i + 5)
                if not first:
                    pe.wait_ge(biased, i)
                for t in range(2):
                    for half in range(2):
                        h = 2 * half + t
                        mm(scores[:, h, :], q_item[:, h, :], k_hi_item[:, :], start=True, stop=False)
                    for half in range(2):
                        h, rows = 2 * half + t, slice(64 * half, 64 * half + 64)
                        ins = mm(scores[:, h, :], q_item[rows, h, :], k_lo_item[rows, :], start=False, stop=True)
                ins.then_inc(scores_done, 1)

            def weigh_values(i, first_block=False, first=False):
                windows = (1,) if first_block else (0, 1)
                count = i + 1 if first_block else 2 * i + 2 - KV_HEADS
                pe.wait_ge(turned_saved, count)
                pe.wait_ge(v_staged, count)
                if not first:
                    pe.wait_ge(attn_gated, i)
                for w in windows:
                    for half in range(2):
                        ins = mm(bank_o[64 * half:64 * half + 64, 0:2 * P], v_item[:, w, :],
                                 probs_t[:, w, 2 * P * half:2 * P * half + 2 * P],
                                 start=(w == windows[0]), stop=(w == 1))
                ins.then_inc(pv_done, 1)

            def turn_probs(i):
                pe.wait_ge(probs_ready, i + 1)
                for h in range(GROUP):
                    ins = nc.tensor.transpose(bank_t[:, 0, h * P:(h + 1) * P], probs[:, 0, h, :], ident[:, :])
                ins.then_inc(turned, 1)

            def item(i, bank, free, count, **last_item):
                score(i, False)
                pe.wait_ge(free, count)
                multiply(T_MA + i, [0], xt_hi, xt_lo, bank[:, :])
                weigh_values(i - 1, **last_item)
                multiply(T_MA + i, [1, 2, 3], xt_hi, xt_lo, bank[:, :])
                turn_probs(i)

            pe.wait_ge(v_saved, KVT)
            score(0, True)
            pe.wait_ge(a_free, A_MA)
            multiply(T_MA, range(4), xt_hi, xt_lo, bank_a[:, :])
            turn_probs(0)
            item(1, bank_b, b_free, B_MA, first_block=True, first=True)
            with pe.Fori(1, KV_HEADS // 2) as n:
                item(2 * n, bank_a, a_free, A_MA + n, first_block=True)
                item(2 * n + 1, bank_b, b_free, B_MA + n, first_block=True)
            item(KV_HEADS, bank_a, a_free, A_MA + KV_HEADS // 2, first_block=True)
            with pe.Fori(KV_HEADS // 2, ITEMS // 2 - 1) as n:
                item(2 * n + 1, bank_b, b_free, B_MA + n)
                item(2 * n + 2, bank_a, a_free, A_MA + 1 + n)
            item(ITEMS - 1, bank_b, b_free, B_MA + ITEMS // 2 - 1)
            multiply(T_X0, [0], xt_hi, xt_lo, bank_s[:, 0, :])
            weigh_values(ITEMS - 1)
            multiply(T_X0, [1, 2, 3], xt_hi, xt_lo, bank_s[:, 0, :])

            pe.wait_ge(ag_lo_ready, AT)
            with pe.Fori(0, KT // 2) as c:
                pe.wait_ge(b_free, B_AO + c)
                multiply(T_AO + c, [0, 1], ag_hi, ag_lo, bank_b[:, :], k_tiles=AT)
                pe.wait_ge(a_free, A_AO + c)
                multiply(T_AO + c, [2, 3], ag_hi, ag_lo, bank_a[:, :], k_tiles=AT)

            def recurrent_gates(c):
                pe.wait_ge(b_free, B_RN + c)
                multiply(T_RN + 2 * c, [0, 1, 2], xt_hi, xt_lo, bank_b[:, :])
                pe.wait_ge(gate_w_lo_ready, c + 1)
                pe.wait_ge(xc_lo_ready, c + 1)
                for n in range(2):
                    mm(bank_s[:, n, :], gate_w_hi[:, n, :], xc_hi[:, :], start=True, stop=False)
                    mm(bank_s[:, n, :], gate_w_hi[:, n, :], xc_lo[:, :], start=False, stop=False)
                    ins = mm(bank_s[:, n, :], gate_w_lo[:, n, :], xc_hi[:, :], start=False, stop=True)
                ins.then_inc(gates_done, 1)
                multiply(T_RN + 2 * c, [3], xt_hi, xt_lo, bank_b[:, :])

            with pe.Fori(0, KT - 1) as c:
                recurrent_gates(c)
                pe.wait_ge(a_free, A_RN + c)
                multiply(T_RN + 1 + 2 * c, range(4), xt_hi, xt_lo, bank_a[:, :])
            recurrent_gates(KT - 1)

            def branch_tile_ready(k):
                pe.wait_ge(hg_lo_ready, KT if k == KT - 1 else KT - 1)

            pe.wait_ge(a_free, A_MX)
            multiply(T_MX, range(4), xt_hi, xt_lo, bank_a[:, :])
            pe.wait_ge(b_free, B_MX)
            multiply(T_MX + 1, range(4), hg_hi, hg_lo, bank_b[:, :], before_tile=branch_tile_ready)
            with pe.Fori(1, KT) as c:
                pe.wait_ge(sig_mr_ready, c)
                multiply(T_MX + 2 * c, range(4), xt_hi, xt_lo, bank_a[:, :])
                pe.wait_ge(mixed_r_ready, c)
                multiply(T_MX + 1 + 2 * c, range(4), hg_hi, hg_lo, bank_b[:, :])

            def output_products(s, k):
                rows = slice(s * P, (s + 1) * P)
                mm(out_banks[s], hg_hi[:, k, rows], xt_hi[:, k, :], start=(k == 0), stop=False)
                mm(out_banks[s], hg_lo[:, k, rows], xt_hi[:, k, :], start=False, stop=False)
                return mm(out_banks[s], hg_hi[:, k, rows], xt_lo[:, k, :], start=False, stop=(k == KT - 1))

            def column_group(g, first=False):
                for pair in range(2):
                    if not first:
                        pe.wait_ge(z_ready, NB * g - NB + 2 * pair + 2)
                    for k in range(KT):
                        if pair == 0:
                            pe.wait_ge(chunk_lo_ready, KT * g + k + 1)
                            if first:
                                pe.wait_ge(mg_lo_ready, k + 1)
                        for s in (2 * pair, 2 * pair + 1):
                            last = output_products(s, k)
                        if pair == 1:
                            last.then_inc(wo_released, 1)
                    if pair == 0:
                        last.then_inc(pair_summed, 1)

            column_group(0, first=True)
            with pe.Fori(1, 3) as g:
                column_group(g)
            for s in range(NB):
                pe.wait_ge(z_ready, NB * 2 + s + 1)
                for k in range(KT):
                    if s == 0:
                        pe.wait_ge(chunk_lo_ready, KT * 3 + k + 1)
                    last = output_products(s, k)
                last.then_inc(rows_summed, 1)


def bucket_row_constants():
    import math

    import numpy as np

    buckets, max_distance, window = 32, 128, 128
    exact = buckets // 2
    rows = np.zeros((buckets + 1, 3 * window), np.float32)
    for t in range(3 * window):
        n = 2 * window - 1 - t
        if not 0 <= n < window:
            b = buckets
        elif n < exact:
            b = n
        else:
            b = min(exact + int(math.log(n / exact) / math.log(max_distance / exact) * (buckets - exact)), buckets - 1)
        rows[b, t] = 1.0
    return rows


def kernel(x, w_in, conv_w, conv_b, w_r, b_r, w_i, b_i, lru_lambda, sinks, w_attn_out, w_rnn_out, w_out,
           ln_g, ln_b, rel_bias):
    import numpy as np
    import concourse.bacc as bacc
    from concourse.bass_utils import run_bass_kernel_spmd

    c = np.ascontiguousarray
    chan = np.concatenate([np.asarray(conv_w)[0], np.asarray(conv_b), np.asarray(b_r), np.asarray(b_i),
                           np.asarray(lru_lambda)])
    chan = c(chan.reshape(8, -1, P).transpose(2, 1, 0))
    arrays = {
        "x_t": c(np.asarray(x)[0].T), "x": c(x), "w_in": c(w_in), "chan": chan, "w_r": c(w_r), "w_i": c(w_i),
        "sinks": c(sinks), "w_attn_out": c(w_attn_out), "w_rnn_out": c(w_rnn_out), "w_out": c(w_out),
        "ln_g": c(ln_g), "ln_b": c(ln_b), "rel_bias": c(rel_bias), "bucket_rows": bucket_row_constants(),
    }
    nc = bacc.Bacc("TRN2", target_bir_lowering=False, num_devices=1)
    args = [nc.dram_tensor(name, a.shape, mybir.dt.from_np(a.dtype), kind="ExternalInput").ap()
            for name, a in arrays.items()]
    out = nc.dram_tensor("out", tuple(np.asarray(x).shape), F32, kind="ExternalOutput").ap()
    hybrid_layer(nc, *args, out)
    r = run_bass_kernel_spmd(nc, [arrays], core_ids=[0])
    return r.results[0]["out"]
```
